# Optimizing a Trainium2 kernel written in Bass

```python
import jax, jax.numpy as jnp
from jax import lax
import numpy as np
import math

D_MODEL = 1024
BATCH = 1
SEQ = 256
DEPTH = 2

HEAD_DIM = 64
N_SB_HEADS = 12
SB_WIDTH = N_SB_HEADS * HEAD_DIM
N_MEM_HEADS = 4
MEM_WIDTH = N_MEM_HEADS * HEAD_DIM
MEM_TOKENS = 256
MIX_WIDTH = SB_WIDTH + MEM_WIDTH
POOL_WINDOWS = (2, 4, 8, 16)
N_POOL_GROUPS = len(POOL_WINDOWS)
POOL_WIDTH = SB_WIDTH
POOL_GROUP = POOL_WIDTH // N_POOL_GROUPS
D_FF = -(-8 * D_MODEL // (3 * 256)) * 256
SB_BLOCK = 128
N_A_LAYERS = DEPTH // 2
N_B_LAYERS = DEPTH - N_A_LAYERS
EPS = 1e-6


def rmsnorm(x, g):
    xf = x.astype(jnp.float32)
    y = xf * lax.rsqrt(jnp.mean(xf * xf, axis=-1, keepdims=True) + EPS)
    return (y * g.astype(jnp.float32)).astype(x.dtype)

def swiglu(h, w_gu, w_down):
    gate, up = jnp.split(h @ w_gu, 2, axis=-1)
    return (jax.nn.silu(gate) * up) @ w_down

def multiscale_pool(u):
    s = u.shape[1]
    uf = u.astype(jnp.float32)
    cs = jnp.cumsum(uf, axis=1)
    pos = jnp.arange(s)
    outs = []
    for g, w in enumerate(POOL_WINDOWS):
        c = cs[..., g * POOL_GROUP:(g + 1) * POOL_GROUP]
        prev = jnp.pad(c, ((0, 0), (w, 0), (0, 0)))[:, :s]
        cnt = jnp.minimum(pos + 1, w).astype(jnp.float32)[None, :, None]
        outs.append((c - prev) / cnt)
    pooled = jnp.concatenate(outs, axis=-1)
    return (pooled - uf).astype(u.dtype)

def memory_kv(mem, mem_norm, w_mem_kv):
    b, m, _ = mem.shape
    k, v = jnp.split(rmsnorm(mem, mem_norm) @ w_mem_kv, 2, axis=-1)
    return (k.reshape(b, m, N_MEM_HEADS, HEAD_DIM), v.reshape(b, m, N_MEM_HEADS, HEAD_DIM))

def memory_attention(q, mk, mv):
    b, s, _ = q.shape
    qh = q.reshape(b, s, N_MEM_HEADS, HEAD_DIM)
    logits = jnp.einsum("bshd,bmhd->bhsm", qh, mk).astype(jnp.float32) * (HEAD_DIM ** -0.5)
    p = jax.nn.softmax(logits, axis=-1).astype(mv.dtype)
    return jnp.einsum("bhsm,bmhd->bshd", p, mv).reshape(b, s, MEM_WIDTH)

def stick_breaking_attention(q, k, v):
    s = q.shape[2]
    scale = HEAD_DIM ** -0.5
    outs = []
    for i in range(s // SB_BLOCK):
        q0 = i * SB_BLOCK
        end = q0 + SB_BLOCK
        qb = q[:, :, q0:end]
        kb = k[:, :, :end]
        vb = v[:, :, :end]
        z = jnp.einsum("bhqd,bhkd->bhqk", qb, kb).astype(jnp.float32) * scale
        tpos = q0 + jnp.arange(SB_BLOCK)
        spos = jnp.arange(end)
        mask = spos[None, :] < tpos[:, None]
        log_not = jnp.where(mask, jax.nn.log_sigmoid(-z), 0.0)
        later = lax.cumsum(log_not, axis=3, reverse=True) - log_not
        wts = jnp.where(mask, jnp.exp(jax.nn.log_sigmoid(z) + later), 0.0)
        outs.append(jnp.einsum("bhqk,bhkd->bhqd", wts.astype(vb.dtype), vb))
    return jnp.concatenate(outs, axis=2)

def pool_layer(x, mem, mem_norm, norm_mix, w_in, w_group, scale, w_mem_kv, w_out, norm_ffn, w_gu, w_down):
    b, s, _ = x.shape
    proj = rmsnorm(x, norm_mix) @ w_in
    u_pool, q_mem = proj[..., :POOL_WIDTH], proj[..., POOL_WIDTH:]
    pooled = multiscale_pool(u_pool).reshape(b, s, N_POOL_GROUPS, POOL_GROUP)
    grouped = jnp.einsum("bsgc,gcd->bsgd", pooled, w_group).reshape(b, s, POOL_WIDTH) * scale
    mk, mv = memory_kv(mem, mem_norm, w_mem_kv)
    mem_out = memory_attention(q_mem, mk, mv)
    x = x + jnp.concatenate([grouped, mem_out], axis=-1) @ w_out
    return x + swiglu(rmsnorm(x, norm_ffn), w_gu, w_down)

def sb_layer(x, mem, k_sh, v_sh, mem_norm, norm_mix, w_q, w_mem_kv, w_out, norm_ffn, w_gu, w_down):
    b, s, _ = x.shape
    proj = rmsnorm(x, norm_mix) @ w_q
    q_sb = proj[..., :SB_WIDTH].reshape(b, s, N_SB_HEADS, HEAD_DIM).transpose(0, 2, 1, 3)
    q_mem = proj[..., SB_WIDTH:]
    sb_out = stick_breaking_attention(q_sb, k_sh, v_sh).transpose(0, 2, 1, 3).reshape(b, s, SB_WIDTH)
    mk, mv = memory_kv(mem, mem_norm, w_mem_kv)
    mem_out = memory_attention(q_mem, mk, mv)
    x = x + jnp.concatenate([sb_out, mem_out], axis=-1) @ w_out
    return x + swiglu(rmsnorm(x, norm_ffn), w_gu, w_down)

def first_inputs(seed: int = 0) -> dict:
    key = jax.random.key(seed)
    ks = jax.random.split(key, 24)
    f32 = jnp.float32
    out_gain = (2.0 * DEPTH) ** -0.5

    def w(k, shape, fan_in, gain=1.0):
        return jax.random.normal(k, shape, f32) * (gain * fan_in ** -0.5)

    def g(k, shape):
        return 1.0 + 0.05 * jax.random.normal(k, shape, f32)

    na, nb = N_A_LAYERS, N_B_LAYERS
    return {
        "x": jax.random.normal(ks[0], (BATCH, SEQ, D_MODEL), f32),
        "mem": jax.random.normal(ks[1], (BATCH, MEM_TOKENS, D_MODEL), f32),
        "mem_norm": g(ks[2], (D_MODEL,)),
        "a_norm_mix": g(ks[3], (na, D_MODEL)),
        "a_w_in": w(ks[4], (na, D_MODEL, MIX_WIDTH), D_MODEL),
        "a_w_group": w(ks[5], (na, N_POOL_GROUPS, POOL_GROUP, POOL_GROUP), POOL_GROUP),
        "a_scale": g(ks[6], (na, POOL_WIDTH)),
        "a_w_mem_kv": w(ks[7], (na, D_MODEL, 2 * MEM_WIDTH), D_MODEL),
        "a_w_out": w(ks[8], (na, MIX_WIDTH, D_MODEL), MIX_WIDTH, out_gain),
        "a_norm_ffn": g(ks[9], (na, D_MODEL)),
        "a_w_gu": w(ks[10], (na, D_MODEL, 2 * D_FF), D_MODEL),
        "a_w_down": w(ks[11], (na, D_FF, D_MODEL), D_FF, out_gain),
        "kv_norm": g(ks[12], (D_MODEL,)),
        "w_kv": w(ks[13], (D_MODEL, 2 * SB_WIDTH), D_MODEL),
        "b_norm_mix": g(ks[14], (nb, D_MODEL)),
        "b_w_q": w(ks[15], (nb, D_MODEL, MIX_WIDTH), D_MODEL),
        "b_w_mem_kv": w(ks[16], (nb, D_MODEL, 2 * MEM_WIDTH), D_MODEL),
        "b_w_out": w(ks[17], (nb, MIX_WIDTH, D_MODEL), MIX_WIDTH, out_gain),
        "b_norm_ffn": g(ks[18], (nb, D_MODEL)),
        "b_w_gu": w(ks[19], (nb, D_MODEL, 2 * D_FF), D_MODEL),
        "b_w_down": w(ks[20], (nb, D_FF, D_MODEL), D_FF, out_gain),
        "final_norm": g(ks[21], (D_MODEL,)),
    }

def first_block(x, mem, mem_norm, a_norm_mix, a_w_in, a_w_group, a_scale, a_w_mem_kv, a_w_out,
              a_norm_ffn, a_w_gu, a_w_down, kv_norm, w_kv, b_norm_mix, b_w_q, b_w_mem_kv,
              b_w_out, b_norm_ffn, b_w_gu, b_w_down, final_norm):
    b, s, _ = x.shape
    k_sh = v_sh = None
    for layer in range(DEPTH):
        if layer < N_A_LAYERS:
            i = layer
            x = pool_layer(x, mem, mem_norm, a_norm_mix[i], a_w_in[i], a_w_group[i], a_scale[i],
                           a_w_mem_kv[i], a_w_out[i], a_norm_ffn[i], a_w_gu[i], a_w_down[i])
        else:
            if layer == N_A_LAYERS:
                kv = rmsnorm(x, kv_norm) @ w_kv
                k_sh = kv[..., :SB_WIDTH].reshape(b, s, N_SB_HEADS, HEAD_DIM).transpose(0, 2, 1, 3)
                v_sh = kv[..., SB_WIDTH:].reshape(b, s, N_SB_HEADS, HEAD_DIM).transpose(0, 2, 1, 3)
            j = layer - N_A_LAYERS
            x = sb_layer(x, mem, k_sh, v_sh, mem_norm, b_norm_mix[j], b_w_q[j], b_w_mem_kv[j],
                         b_w_out[j], b_norm_ffn[j], b_w_gu[j], b_w_down[j])
    return rmsnorm(x, final_norm)


DEPTH_2 = 1

PLE_DIM = 256
RMS_EPS = 1e-6
A_HEAD_DIM = 64
A_HEADS = D_MODEL // 128
A_WIDTH = A_HEADS * A_HEAD_DIM
MOBA_BLOCK = 256
MOBA_TOPK = 3
Q_CHUNK = 16
REL_BUCKETS = 32
REL_MAX_EXACT = REL_BUCKETS // 2
REL_MAX_DIST = 128
B_HEAD_DIM = 64
B_HEADS = D_MODEL // 128
B_WIDTH = B_HEADS * B_HEAD_DIM
DECAY_RANK = 64
ICLR_RANK = 64
GN_EPS = 64e-5
A_COLS = 4 * A_WIDTH
RW_COLS = 4 * B_WIDTH + DECAY_RANK + ICLR_RANK
IN_COLS = A_COLS + RW_COLS + 2 * D_MODEL


def _rms_norm(x, g):
    xf = x.astype(jnp.float32)
    y = xf * lax.rsqrt(jnp.mean(xf * xf, axis=-1, keepdims=True) + RMS_EPS)
    return y * g.astype(jnp.float32)

def _t5_bucket(dist):
    n = jnp.maximum(dist, 0)
    nf = jnp.maximum(n, 1).astype(jnp.float32)
    large = REL_MAX_EXACT + (jnp.log(nf / REL_MAX_EXACT) / math.log(REL_MAX_DIST / REL_MAX_EXACT)
                             * (REL_BUCKETS - REL_MAX_EXACT)).astype(jnp.int32)
    large = jnp.minimum(large, REL_BUCKETS - 1)
    return jnp.where(n < REL_MAX_EXACT, n, large)

def _moba_attention(q, k, v, rel_bias):
    bsz, seq, nh, hd = q.shape
    n_blk = -(-seq // MOBA_BLOCK)
    pad = n_blk * MOBA_BLOCK - seq
    topk = min(MOBA_TOPK, n_blk)
    qh = jnp.swapaxes(q, 1, 2).astype(jnp.float32) * (hd ** -0.5)
    kh = jnp.pad(jnp.swapaxes(k, 1, 2).astype(jnp.float32), ((0, 0), (0, 0), (0, pad), (0, 0)))
    vh = jnp.pad(jnp.swapaxes(v, 1, 2).astype(jnp.float32), ((0, 0), (0, 0), (0, pad), (0, 0)))
    k_blk = kh.reshape(bsz, nh, n_blk, MOBA_BLOCK, hd)
    v_blk = vh.reshape(bsz, nh, n_blk, MOBA_BLOCK, hd)
    k_mean = jnp.mean(k_blk, axis=3)
    gate = jnp.einsum('bhsd,bhnd->bhsn', qh, k_mean)
    q_blk = jnp.arange(seq) // MOBA_BLOCK
    past = jnp.arange(n_blk)[None, :] < q_blk[:, None]
    gate = jnp.where(past[None, None], gate, -jnp.inf)
    _, sel = lax.top_k(gate, topk)
    bias_h = rel_bias.T.astype(jnp.float32)
    b_idx = jnp.arange(bsz)[:, None, None, None]
    h_idx = jnp.arange(nh)[None, :, None, None]
    offs = jnp.arange(MOBA_BLOCK)

    def chunk(c):
        t0 = c * Q_CHUNK
        pos = t0 + jnp.arange(Q_CHUNK)
        qb = t0 // MOBA_BLOCK
        qc = lax.dynamic_slice_in_dim(qh, t0, Q_CHUNK, axis=2)
        sc = lax.dynamic_slice_in_dim(sel, t0, Q_CHUNK, axis=2)
        ks = k_blk[b_idx, h_idx, sc]
        vs = v_blk[b_idx, h_idx, sc]
        key_pos = sc[..., None] * MOBA_BLOCK + offs
        dist = pos[None, None, :, None, None] - key_pos
        l_sel = jnp.einsum('bhqd,bhqkjd->bhqkj', qc, ks) + bias_h[h_idx[..., None], _t5_bucket(dist)]
        valid = (sc < qb)[..., None]
        l_sel = jnp.where(valid, l_sel, -jnp.inf).reshape(bsz, nh, Q_CHUNK, topk * MOBA_BLOCK)
        ko = lax.dynamic_index_in_dim(k_blk, qb, axis=2, keepdims=False)
        vo = lax.dynamic_index_in_dim(v_blk, qb, axis=2, keepdims=False)
        dist_o = pos[:, None] - (qb * MOBA_BLOCK + offs)[None, :]
        l_own = jnp.einsum('bhqd,bhjd->bhqj', qc, ko) + bias_h[:, _t5_bucket(dist_o)][None]
        l_own = jnp.where((dist_o >= 0)[None, None], l_own, -jnp.inf)
        probs = jax.nn.softmax(jnp.concatenate([l_sel, l_own], axis=-1), axis=-1)
        p_sel = probs[..., :topk * MOBA_BLOCK].reshape(bsz, nh, Q_CHUNK, topk, MOBA_BLOCK)
        p_own = probs[..., topk * MOBA_BLOCK:]
        return (jnp.einsum('bhqkj,bhqkjd->bhqd', p_sel, vs)
                + jnp.einsum('bhqj,bhjd->bhqd', p_own, vo))

    outs = lax.map(chunk, jnp.arange(seq // Q_CHUNK))
    return outs.transpose(1, 0, 3, 2, 4).reshape(bsz, seq, nh * hd)

def _rwkv7_time_mix(cols, mu, w0, w_up, a0, a_up, k_k, k_a, r_k, ln_w, ln_b):
    bsz, seq, _ = cols.shape
    cols = cols.astype(jnp.float32)
    prev = jnp.pad(cols, ((0, 0), (1, 0), (0, 0)))[:, :-1]
    cols = cols + (prev - cols) * mu.astype(jnp.float32)
    o = np.cumsum([0, B_WIDTH, B_WIDTH, B_WIDTH, B_WIDTH, DECAY_RANK])
    r, k, v, z = (cols[..., o[j]:o[j + 1]] for j in range(4))
    wd = cols[..., o[4]:o[5]]
    ad = cols[..., o[5]:]
    w_log = -jax.nn.softplus(-(w0 + jnp.tanh(wd) @ w_up)) - 0.5
    decay = jnp.exp(-jnp.exp(w_log))
    a = jax.nn.sigmoid(a0 + ad @ a_up)
    heads = lambda t: t.reshape(bsz, seq, B_HEADS, B_HEAD_DIM)
    kk = heads(k * k_k)
    kk = kk / jnp.maximum(jnp.linalg.norm(kk, axis=-1, keepdims=True), 1e-12)
    k = k * (1.0 + (a - 1.0) * k_a)
    rh, kh, vh, ah = heads(r), heads(k), heads(v), heads(a)
    xs = tuple(jnp.moveaxis(t, 1, 0) for t in (rh, heads(decay), kh, vh, -kk, kk * ah))

    def step(state, inp):
        r_t, w_t, k_t, v_t, a_t, b_t = inp
        sa = jnp.einsum('bhvk,bhk->bhv', state, a_t)
        state = (state * w_t[:, :, None, :] + sa[..., None] * b_t[:, :, None, :]
                 + v_t[..., None] * k_t[:, :, None, :])
        return state, jnp.einsum('bhvk,bhk->bhv', state, r_t)

    s0 = jnp.zeros((bsz, B_HEADS, B_HEAD_DIM, B_HEAD_DIM), jnp.float32)
    _, y = lax.scan(step, s0, xs)
    y = jnp.moveaxis(y, 0, 1)
    mean = jnp.mean(y, axis=-1, keepdims=True)
    var = jnp.mean(jnp.square(y - mean), axis=-1, keepdims=True)
    y = ((y - mean) * lax.rsqrt(var + GN_EPS)).reshape(bsz, seq, B_WIDTH) * ln_w + ln_b
    bonus = jnp.sum(rh * kh * r_k, axis=-1, keepdims=True) * vh
    y = y + bonus.reshape(bsz, seq, B_WIDTH)
    return y, z

def second_inputs(seed: int = 0) -> dict:
    key = jax.random.key(seed)
    ks = jax.random.split(key, 22)
    n = lambda k, s, sc: jax.random.normal(k, s, jnp.float32) * sc
    L = DEPTH_2
    return {
        "x": n(ks[0], (BATCH, SEQ, D_MODEL), 1.0),
        "p": n(ks[1], (DEPTH_2, BATCH, SEQ, PLE_DIM), 1.0),
        "g_pre": 1.0 + n(ks[2], (L, D_MODEL), 0.05),
        "w_in": n(ks[3], (L, D_MODEL, IN_COLS), D_MODEL ** -0.5),
        "rel_bias": n(ks[4], (REL_BUCKETS, A_HEADS), 0.5),
        "mu_shift": jax.random.uniform(ks[5], (L, RW_COLS), jnp.float32, 0.0, 1.0),
        "w0": jax.random.uniform(ks[6], (L, B_WIDTH), jnp.float32, -4.0, 1.0),
        "w_up": n(ks[7], (L, DECAY_RANK, B_WIDTH), 0.5 * DECAY_RANK ** -0.5),
        "a0": n(ks[8], (L, B_WIDTH), 0.5),
        "a_up": n(ks[9], (L, ICLR_RANK, B_WIDTH), 0.5 * ICLR_RANK ** -0.5),
        "k_k": 0.85 + n(ks[10], (L, B_WIDTH), 0.05),
        "k_a": 1.0 + n(ks[11], (L, B_WIDTH), 0.05),
        "r_k": n(ks[12], (L, B_HEADS, B_HEAD_DIM), 0.1),
        "ln_x_w": 1.0 + n(ks[13], (L, B_WIDTH), 0.05),
        "ln_x_b": n(ks[14], (L, B_WIDTH), 0.02),
        "p_a": n(ks[15], (L, A_WIDTH, D_MODEL), A_WIDTH ** -0.5),
        "p_b": n(ks[16], (L, B_WIDTH, D_MODEL), B_WIDTH ** -0.5),
        "w_out": n(ks[17], (L, D_MODEL, D_MODEL), D_MODEL ** -0.5),
        "g_post": 1.0 + n(ks[18], (L, D_MODEL), 0.05),
        "w_ple_up": n(ks[19], (L, PLE_DIM, D_MODEL), PLE_DIM ** -0.5),
        "w_ple_gate": n(ks[20], (L, D_MODEL, D_MODEL), D_MODEL ** -0.5),
    }

def second_block(x, p, g_pre, w_in, rel_bias, mu_shift, w0, w_up, a0, a_up, k_k, k_a, r_k,
              ln_x_w, ln_x_b, p_a, p_b, w_out, g_post, w_ple_up, w_ple_gate):
    bsz, seq, _ = x.shape
    h = x.astype(jnp.float32)
    for i in range(DEPTH_2):
        u = _rms_norm(h, g_pre[i]).astype(w_in.dtype)
        cols = u @ w_in[i]
        a_cols = cols[..., :A_COLS]
        b_cols = cols[..., A_COLS:A_COLS + RW_COLS]
        gate_a = cols[..., A_COLS + RW_COLS:A_COLS + RW_COLS + D_MODEL].astype(jnp.float32)
        gate_b = cols[..., A_COLS + RW_COLS + D_MODEL:].astype(jnp.float32)
        qa, ka, va, za = (a_cols[..., j * A_WIDTH:(j + 1) * A_WIDTH].reshape(bsz, seq, A_HEADS, A_HEAD_DIM)
                          for j in range(4))
        y_a = _moba_attention(qa, ka, va, rel_bias) * jax.nn.silu(za.reshape(bsz, seq, A_WIDTH).astype(jnp.float32))
        y_b, z_b = _rwkv7_time_mix(b_cols, mu_shift[i], w0[i], w_up[i], a0[i], a_up[i], k_k[i], k_a[i],
                                   r_k[i], ln_x_w[i], ln_x_b[i])
        y_b = y_b * jax.nn.silu(z_b)
        merged = (jax.nn.sigmoid(gate_a) * (y_a.astype(p_a.dtype) @ p_a[i])
                  + jax.nn.sigmoid(gate_b) * (y_b.astype(p_b.dtype) @ p_b[i]))
        y = merged.astype(w_out.dtype) @ w_out[i]
        h = h + _rms_norm(y, g_post[i])
        e = p[i] @ w_ple_up[i]
        h = h + jax.nn.sigmoid((h.astype(w_ple_gate.dtype) @ w_ple_gate[i]).astype(jnp.float32)) * e
    return h.astype(x.dtype)


def setup_inputs(seed=0):
    out = dict(first_inputs(seed))
    for name, value in second_inputs(seed + 1).items():
        if name != "x":
            out[name + "_2"] = value
    return out


def reference(
    x, mem, mem_norm, a_norm_mix, a_w_in, a_w_group, a_scale, a_w_mem_kv, a_w_out, a_norm_ffn,
    a_w_gu, a_w_down, kv_norm, w_kv, b_norm_mix, b_w_q, b_w_mem_kv, b_w_out, b_norm_ffn, b_w_gu,
    b_w_down, final_norm, p_2, g_pre_2, w_in_2, rel_bias_2, mu_shift_2, w0_2, w_up_2, a0_2,
    a_up_2, k_k_2, k_a_2, r_k_2, ln_x_w_2, ln_x_b_2, p_a_2, p_b_2, w_out_2, g_post_2,
    w_ple_up_2, w_ple_gate_2,
):
    x = first_block(
        x, mem, mem_norm, a_norm_mix, a_w_in, a_w_group, a_scale, a_w_mem_kv, a_w_out,
        a_norm_ffn, a_w_gu, a_w_down, kv_norm, w_kv, b_norm_mix, b_w_q, b_w_mem_kv, b_w_out,
        b_norm_ffn, b_w_gu, b_w_down, final_norm,
    )
    return second_block(
        x, p_2, g_pre_2, w_in_2, rel_bias_2, mu_shift_2, w0_2, w_up_2, a0_2, a_up_2, k_k_2,
        k_a_2, r_k_2, ln_x_w_2, ln_x_b_2, p_a_2, p_b_2, w_out_2, g_post_2, w_ple_up_2,
        w_ple_gate_2,
    )


_drawn_inputs = setup_inputs


def setup_inputs(seed=0):
    import zlib

    import numpy as np

    out = dict(_drawn_inputs(seed))
    spreads = {}
    factors = {'mem_norm': 8.0,
     'b_norm_mix': 6.059,
     'k_k_2': 13.474,
     'ln_x_b_2': 4.283,
     'kv_norm': 3.185,
     'b_norm_ffn': 4.811}
    for name, (base, spread) in spreads.items():
        noise = np.random.default_rng([zlib.crc32(name.encode()), seed]).standard_normal(out[name].shape)
        drawn = base * np.exp(spread * noise) if base else spread * noise
        out[name] = __import__('jax').numpy.asarray(drawn.astype(out[name].dtype))
    for name, factor in factors.items():
        out[name] = (out[name] * factor).astype(out[name].dtype)
    return out
```

```python
from contextlib import ExitStack

import numpy as np

import concourse.bass as bass
from concourse import mybir
from concourse.alu_op_type import AluOpType as ALU

ACT = mybir.ActivationFunctionType
F32 = mybir.dt.float32
F32R = mybir.dt.float32r
AX_X = mybir.AxisListType.X

P = 128
D = 1024
T = 256
KD = D // P
HALF = 64
NSB = 12
SBT = NSB * HALF // P
FF = 2816
KF = FF // P
EPS = 1e-6
NEG = -1.0e30
SCALE = HALF ** -0.5
DECAY = float(np.exp(-0.5))
CHUNK = 64
GN_EPS = 64e-5

U_MEMA = 0
U_IN = 2
U_MEMB = 6
U_OUTA = 8
U_GUA = 12
N_GU = KF
U_DNA = U_GUA + N_GU
N_DN = 2 * KD
U_K = U_DNA + N_DN
SB_ORDER = "kkvqqvkqvm"
K_UNITS, Q_UNITS, V_UNITS, M_UNITS = (tuple(U_K + n for n, c in enumerate(SB_ORDER) if c == kind) for kind in "kqvm")
SB_BEFORE, SB_AFTER = (0, 1), (4, 5, 8, 10)
U_OUTB = U_K + len(SB_ORDER)
U_GUB = U_OUTB + 4
U_DNB = U_GUB + N_GU
U_RW = U_DNB + N_DN
U_LR = U_RW + 8
U_QA = U_LR + 1
U_KA = U_QA + 2
U_VA = U_KA + 2
U_ZA = U_VA + 2
U_GATE = U_ZA + 2
U_PAB = U_GATE + 8
U_OUT2 = U_PAB + 4
U_EUP = U_OUT2 + 4
U_EGATE = U_EUP + 1
N_UNITS = U_EGATE + 4
UNIT = 16 * P
DN_TILES = KF // 2

RAW_SLOTS = 4
SPLIT_SLOTS = 2


def first_group(u):
    g = u
    for u0 in (U_DNA, U_DNB):
        g -= max(0, min(u - u0, N_DN)) - max(0, min(u - u0, N_DN)) // 2
    g += max(0, min(u - U_PAB, 4)) + 3 * max(0, min(u - U_EUP, 1))
    return g


VEC = {}
_at = 0
for _name, _n in [("mem_norm", 8), ("a_norm_mix", 8), ("a_norm_ffn", 8), ("kv_norm", 8), ("b_norm_mix", 8),
                  ("b_norm_ffn", 8), ("final_norm", 8), ("g_pre_2", 8), ("g_post_2", 8), ("a_scale", 6),
                  ("mu_shift_2", 17), ("w0_2", 4), ("a0_2", 4), ("k_k_2", 4), ("k_a_2", 4), ("r_k_2", 4),
                  ("ln_x_w_2", 4), ("ln_x_b_2", 4)]:
    VEC[_name] = _at
    _at += _n
N_VEC = _at

MASKS = ["strict_lower", "strict_upper", "upper", "pair_lower", "pair_upper",
         "join2", "join4", "join8", "join16", "join32", "heads", "carry0", "carry1"]
N_MASK = len(MASKS)


def masks():
    r, c = np.indices((P, P))
    same = r // CHUNK == c // CHUNK
    out = [same & (r > c), same & (r < c), same & (r <= c),
           (r // 2 == c // 2) & (r > c), (r // 2 == c // 2) & (r < c)]
    for b in (2, 4, 8, 16, 32):
        out.append((r // (2 * b) == c // (2 * b)) & (r % (2 * b) < b) & (c % (2 * b) >= b))
    out.append(r // HALF == c // HALF)
    carry = c % CHUNK != 0
    out += [carry, carry]
    return np.stack(out, 1).astype(np.float32)


def buckets():
    n = np.arange(T)
    nf = np.maximum(n, 1).astype(np.float32)
    large = 16 + (np.log(nf / 16) / np.float32(np.log(128 / 16)) * 16).astype(np.int32)
    bucket = np.where(n < 16, n, np.minimum(large, 31))
    out = np.zeros((32, T), np.float32)
    out[bucket[T - 1 - n], n] = 1
    return out


def program(nc, io, out):
    ctx = ExitStack()
    with ctx:
        def sem(name):
            return ctx.enter_context(nc.semaphore(name))

        def sb(name, shape, dt=F32, scope=None):
            return (scope or ctx).enter_context(nc.sbuf_tensor(name, shape, dt))

        raw = sb("raw", [P, RAW_SLOTS, UNIT])
        hi = sb("hi", [P, SPLIT_SLOTS, UNIT], F32R)
        lo = sb("lo", [P, SPLIT_SLOTS, UNIT], F32R)
        X = sb("X", [P, KD, T])
        XH = sb("XH", [P, KD, T], F32R)
        XL = sb("XL", [P, KD, T], F32R)
        vec = sb("vec", [P, N_VEC])
        gfp = sb("gfp", [P, KD])
        RS = sb("RS", [P, 2, 2, T])
        RSC = sb("RSC", [P, 2, 2])
        RV = sb("RV", [P, T + 2])
        ACC = sb("ACC", [P, 2, T])
        SQT = sb("SQT", [P, 2, T])
        ident = sb("ident", [P, P])
        ones = sb("ones", [P, P])
        PR = sb("PR", [P, 2, 2, T])
        PTS = sb("PTS", [P, 2, 2, T])
        MX = sb("MX", [P, 2, 2])
        NM = sb("NM", [P, 2, 2])
        SM = sb("SM", [P, 2, 2])
        RC = sb("RC", [P, 2, 2])

        block1 = ExitStack()
        HH = sb("HH", [P, KF, T], F32R, block1)
        HL = sb("HL", [P, KF, T], F32R, block1)
        MK = sb("MK", [P, 2, 2, T], F32, block1)
        MV = sb("MV", [P, 2, 2, T], F32, block1)
        QM = sb("QM", [P, 2, T], F32, block1)
        nones = sb("nones", [P, P], F32, block1)
        ntri = sb("ntri", [P, P], F32, block1)
        before = sb("before", [P, 2 * P], F32, block1)
        notbefore = sb("notbefore", [P, 3 * P], F32, block1)
        GU = sb("GU", [P, 2, 2, T], F32, block1)
        SG = sb("SG", [P, 2, T], F32, block1)
        layer_a = ExitStack()
        MEM = sb("MEM", [P, KD, T], F32, layer_a)
        PADW = T + 16
        UP = sb("UP", [P, 6, PADW], F32, layer_a)
        SA = sb("SA", [P, 6, PADW], F32, layer_a)
        SB = sb("SB", [P, 6, PADW], F32, layer_a)
        INV = sb("INV", [P, 4, T], F32, layer_a)
        WG = sb("WG", [P, 8, 192], F32, layer_a)
        layer_a.close()
        OH = GU[0:32, 0, 0, :]
        RB = SG[0:32, 0, 0:8]
        RBX = PR[0:32, :, :, :].rearrange("p a i c -> p (a i c)").rearrange("p (h c) -> p h c", h=8)
        STAGE = [a[:, :, :].rearrange("p a b -> p (a b)")[:, 0:4 * T].rearrange("p (h c) -> p h c", h=2)
                 for a in (UP, SA, SB, INV)]
        block2 = ctx
        layer_b = ExitStack()
        KT = sb("KT", [P, SBT, T], F32, layer_b)
        QT = sb("QT", [P, SBT, T], F32, layer_b)
        V = sb("V", [P, 2, NSB * HALF], F32, layer_b)
        LG = sb("LG", [P, 2, 3 * P], F32, layer_b)
        SP = sb("SP", [P, 2, 3 * P], F32, layer_b)
        WT = sb("WT", [P, 2, 3 * P], F32, layer_b)
        layer_b.close()
        block1.close()

        C = sb("C", [P, 17, T + 1], F32, block2)
        AI = sb("AI", [P, 4, T], F32, block2)
        KK = sb("KK", [P, 4, T], F32, block2)
        BON = sb("BON", [P, 4, T], F32, block2)
        SGT = sb("SGT", [P, 16, T], F32, block2)
        YAH = sb("YAH", [P, 4, T], F32R, block2)
        YAL = sb("YAL", [P, 4, T], F32R, block2)
        ZA = sb("ZA", [P, 4, T], F32, block2)
        VA = sb("VA", [P, 2, 512], F32, block2)
        ED = sb("ED", [P, 4, 4], F32, block2)
        cmask = sb("cmask", [P, N_MASK, P], F32, block2)
        low_up = sb("low_up", [P, 512], F32, block2)
        own = ExitStack()
        QA = sb("QA", [P, 4, T], F32, own)
        KA = sb("KA", [P, 4, T], F32, own)
        BI = sb("BI", [P, 2, 2, T], F32, own)
        own.close()
        YBH = sb("YBH", [P, 4, T], F32R, block2)
        YBL = sb("YBL", [P, 4, T], F32R, block2)
        BI_pad = sb("BI_pad", [P, 2, 2, T], F32, block2)
        prep = ExitStack()
        TMP = sb("TMP", [P, 4, T], F32, prep)
        SW = sb("SW", [P, 4, T], F32, prep)
        CUM = sb("CUM", [P, 4, T], F32, prep)
        prep.close()
        mats = ExitStack()
        TOK = sb("TOK", [P, 3, 2, P], F32, mats)
        RHS = sb("RHS", [P, 2, 2, P], F32, mats)
        AM = sb("AM", [P, 2, 2, P], F32, mats)
        MM = sb("MM", [P, 2, 2, P], F32, mats)
        NN = sb("NN", [P, 2, 2, P], F32, mats)
        LK = sb("LK", [P, 2, 2, P], F32, mats)
        MB = sb("MB", [P, 2, 2, P], F32, mats)
        MC = sb("MC", [P, 2, 2, P], F32, mats)
        YM = sb("YM", [P, 2, 2, P], F32, mats)
        TTS = sb("TTS", [P, HALF], F32, mats)
        mats.close()
        MAT = PTS[:, 0, 0, :]
        YQ = PTS[:, 0, 1, :]
        SAO = PTS[:, 1, 0, :].rearrange("p (h i c) -> p h i c", h=2, i=2)
        GT = PR[:, 0, :, :].rearrange("p a b -> p (a b)")[:, 0:6 * HALF].rearrange("p (c g v) -> p c g v", c=3, g=2)
        TTB = PR[:, 1, :, :].rearrange("p a (c v) -> p (a c) v", v=P)
        late = ExitStack()
        PIN = sb("PIN", [P, 2, T], F32, late)
        PH = sb("PH", [P, 2, T], F32R, late)
        PL = sb("PL", [P, 2, T], F32R, late)
        SIG = sb("SIG", [P, 2, 2, T], F32, late)
        late.close()

        ps = [ctx.enter_context(nc.psum_tensor(f"ps{i}", [P, 512], F32)) for i in range(8)]
        PROJ, STAT, LOG, TRA, OUTP = ps[0:2], ps[2], ps[3:5], ps[5], ps[6:8]

        loaded = [sem(f"loaded{i}") for i in range(RAW_SLOTS)]
        vecs_in, x_in, mem_in, group_in = sem("vecs_in"), sem("x_in"), sem("mem_in"), sem("group_in")
        hi_ready, lo_ready = sem("hi_ready"), sem("lo_ready")
        unit_done = sem("unit_done")
        evac_done = sem("evac_done")
        x_done = sem("x_done")
        xh_ready, xl_ready = sem("xh_ready"), sem("xl_ready")
        mh_ready, ml_ready = sem("mh_ready"), sem("ml_ready")
        hh_ready, hl_ready = sem("hh_ready"), sem("hl_ready")
        eh_ready, el_ready = sem("eh_ready"), sem("el_ready")
        gate_in, silu_done, h_done = sem("gate_in"), sem("silu_done"), sem("h_done")
        sq_done, stat_done, rv_done, rs_done = sem("sq_done"), sem("stat_done"), sem("rv_done"), sem("rs_done")
        const_done = sem("const_done")
        pool_chain, dve_chain, act_chain = sem("pool_chain"), sem("dve_chain"), sem("act_chain")
        att_logits, att_max, att_exp, att_norm = sem("att_logits"), sem("att_max"), sem("att_exp"), sem("att_norm")
        att_turned, att_copied, att_pv, att_out = sem("att_turned"), sem("att_copied"), sem("att_pv"), sem("att_out")
        pads_done, inv_done, pooled_done = sem("pads_done"), sem("inv_done"), sem("pooled_done")
        grouped_done, grouped_free = sem("grouped_done"), sem("grouped_free")
        sb_z, sb_abs, sb_exp, sb_ln, sb_sp = sem("sb_z"), sem("sb_abs"), sem("sb_exp"), sem("sb_ln"), sem("sb_sp")
        sb_cum, sb_arg, sb_wt, sb_pv, sb_out = sem("sb_cum"), sem("sb_arg"), sem("sb_wt"), sem("sb_pv"), sem("sb_out")
        stored = sem("stored")
        filled, taken = [sem(f"filled{b}") for b in range(8)], [sem(f"taken{b}") for b in range(8)]
        table_stored, table_in = sem("table_stored"), sem("table_in")
        masks_in, low_in, buckets_in, table_done, table_out = (sem("masks_in"), sem("low_in"), sem("buckets_in"),
                                                               sem("table_done"), sem("table_out"))
        bias_in = [sem("bias_in0"), sem("bias_in1")]
        bias_half = bias_in
        h_ready, rsp_done, shifted, tanh_done, cum_done = (sem("h_ready"), sem("rsp_done"), sem("shifted"),
                                                           sem("tanh_done"), sem("cum_done"))
        kk_sq, kk_rv, kk_rn, bon_in, exp_done = sem("kk_sq"), sem("kk_rv"), sem("kk_rn"), sem("bon_in"), sem("exp_done")
        hats_done, own_max, own_exp, own_norm = sem("hats_done"), sem("own_max"), sem("own_exp"), sem("own_norm")
        own_y, yah_ready, yal_ready = sem("own_y"), sem("yah_ready"), sem("yal_ready")
        za_in, za_done, z_done, gates_in, gates_done = (sem("za_in"), sem("za_done"), sem("z_done"), sem("gates_in"),
                                                        sem("gates_done"))
        state_done, inverse_done, gn_sq, gn_rv, gn_rs = (sem("state_done"), sem("inverse_done"), sem("gn_sq"),
                                                         sem("gn_rv"), sem("gn_rs"))
        e_part = sem("e_part")
        y_out = sem("y_out")
        yb_done, ybh_ready, ybl_ready, merged = sem("yb_done"), sem("ybh_ready"), sem("ybl_ready"), sem("merged")
        y_done, p_in, ph_ready, pl_ready, sig_done, out_ready = (sem("y_done"), sem("p_in"), sem("ph_ready"),
                                                                 sem("pl_ready"), sem("sig_done"), sem("out_ready"))

        table = nc.dram_tensor("bias_table", (8, P, 2 * T), F32).ap()
        block = ctx.enter_context(nc.Block())

        def need(eng, semaphore, count):
            if not isinstance(count, int) or count > 0:
                eng.wait_ge(semaphore, count)

        def over_units(eng, u0, n, body):
            if n >= 8:
                with eng.Fori(0, n // 4) as i:
                    for j in range(4):
                        body(i * 4 + (u0 + j), (u0 + j) % 4)
                done = n - n % 4
            else:
                done = 0
            for j in range(done, n):
                body(u0 + j, (u0 + j) % 4)

        def width(u):
            return DN_TILES * P if U_DNA <= u < U_DNA + N_DN or U_DNB <= u < U_DNB + N_DN else UNIT

        HEADS = {"mem_a": 0, "mem_b": 4, "own": 8}

        plan = [("consts",), ("split", 0), ("split", 1), ("mem_in",), ("norm_mem",)]
        plan += [("unit_mk", 0), ("x_in",), ("unit_mv", 1), ("table",), ("stats", 1, 0), ("unit_qm", U_IN), ("pads",)]
        plan += [("unit_pool", U_IN + 1), ("logits", 0), ("logits", 1), ("soft", 0)]
        plan += [("unit_pool", U_IN + 2), ("turn", 0), ("logits", 2), ("soft", 1), ("pv", 0), ("turn", 1)]
        plan += [("unit_pool", U_IN + 3), ("logits", 3), ("soft", 2), ("pool",), ("pv", 1), ("turn", 2), ("unit_mk", U_MEMB),
                 ("soft", 3), ("pv", 2), ("turn", 3), ("pv", 3), ("unit_mv", U_MEMB + 1), ("grouped",)]
        plan += [("unit_out", U_OUTA + j) for j in range(4)]
        plan += [("xsplit", 0), ("gu", U_GUA), ("down", U_DNA)]
        units = [({"k": "unit_k", "q": "unit_q", "v": "unit_v", "m": "unit_qm"}[c], U_K + n) for n, c in enumerate(SB_ORDER)]
        plan += [units.pop(0), ("stats", 3, 1), units.pop(0), ("esplit", 0), ("esplit", 1), units.pop(0), units.pop(0),
                 ("log_table",), ("sbz", 0), ("sbz", 1)]
        for h in range(NSB):
            plan += [units.pop(0) for _ in range(SB_BEFORE.count(h))]
            plan += [("sbcum", h)] + ([("sbz", h + 2)] if h + 2 < NSB else [])
            plan += [units.pop(0) for _ in range(SB_AFTER.count(h))]
            plan += [("sbpv", h)] if h > 1 else [("sbpv", 0), ("sbpv", 1)] if h else []
        plan += [("logits", 4), ("logits", 5), ("soft", 4), ("turn", 4), ("logits", 6), ("soft", 5), ("pv", 4), ("turn", 5),
                 ("logits", 7), ("soft", 6), ("pv", 5), ("turn", 6), ("soft", 7), ("pv", 6), ("turn", 7), ("pv", 7)]
        plan += [("unit_out", U_OUTB + j) for j in range(4)]
        plan += [("xsplit", 1), ("gu", U_GUB), ("down", U_DNB)]

        LOG0, LOG1, TR, OUT0, OUT1, ST = 3, 4, 5, 6, 7, 2

        def turns():
            return [0] * 8

        def mask(name, a=None, b=None):
            m = cmask[:, MASKS.index(name):MASKS.index(name) + 1, :]
            if b is not None:
                return m.unsqueeze(1).to_broadcast([P, a, b, P])
            return m if a is None else m.to_broadcast([P, a, P])

        second = [("stats", 5, 1), ("h",), ("rw_first",)]
        second += [("unit_rw", U_RW + 2), ("shift", 0), ("unit_rw", U_RW + 3), ("unit_rw", U_RW + 4), ("shift", 1),
                   ("unit_rw", U_RW + 5), ("unit_rw", U_RW + 6), ("shift", 2), ("unit_rw", U_RW + 7), ("unit_lr", U_LR),
                   ("unit_qa", U_QA), ("shift", 3), ("shift", 4), ("unit_qa", U_QA + 1), ("low",), ("kk",),
                   ("unit_ka", U_KA), ("bonus",), ("unit_ka", U_KA + 1), ("exps",), ("unit_va", U_VA), ("unit_va", U_VA + 1),
                   ("unit_za", U_ZA), ("unit_za", U_ZA + 1)]
        gates = [("unit_gate", U_GATE + j) for j in range(8)]
        for h in range(8):
            second += [("mlog", h)]
            if h:
                second += [("mturn", h - 1)]
            second += [("msoft", h)]
            if h:
                second += [("mpv", h - 1)]
        second += [("mturn", 7), ("mpv", 7)]
        for ct in range(4):
            last = ct - 1
            second += [("tok", ct), gates.pop(0), ("grams", ct), gates.pop(0), ("lv", ct)]
            for level in range(5):
                second += [("level", ct, level)]
                if ct and level < 3:
                    second += [(("gn", "gn2", "gn3")[level], last)]
            second += [("apply", ct), ("chunks", ct)]
            second += [("scan", ct, 1), ("scan", ct, 2), ("scan", ct, 3), ("sa", ct), ("yt", ct)]
        second += [("gn", 3), ("gn2", 3), ("gn3", 3)]
        second += [("unit_pab", U_PAB + j) for j in range(4)]
        second += [("unit_out2", U_OUT2 + j) for j in range(4)]
        second += [("p_in",), ("stats", 7, 0), ("unit_eup", U_EUP), ("post",)]
        second += [("unit_egate", U_EGATE + j) for j in range(4)]
        plan += second

        def run(handlers):
            for name, *args in plan:
                if name in handlers:
                    handlers[name](*args)

        @block.sync
        def _(sp):
            sp.dma_start(vec[:, :], io["vec"]).then_inc(vecs_in, 16)
            sp.dma_start(MEM[:, :, :], io["mem"]).then_inc(mem_in, 16)

            def load(u, s, n):
                if not isinstance(u, int) or u >= RAW_SLOTS:
                    sp.wait_ge(hi_ready, u * 2 - 6)
                    sp.wait_ge(lo_ready, u * 2 - 6)
                sp.dma_start(raw[:, s, 0:n], src_of(u, n)).then_inc(loaded[s], 16)

            def src_of(u, n):
                if n == UNIT:
                    dn = 0
                    if isinstance(u, int):
                        dn = max(0, min(u - U_DNA, N_DN)) + max(0, min(u - U_DNB, N_DN))
                        return io["wide"][u - dn, :, :]
                    return io["wide"][bass.ds(u - offset[0], 1), :, :].rearrange("o p n -> p (o n)")
                return io["down"][bass.ds(u - offset[0], 1), :, :].rearrange("o p n -> p (o n)")

            offset = [0]
            load(0, 0, UNIT)
            sp.dma_start(X[:, :, :], io["x"]).then_inc(x_in, 16)
            for u in range(1, 4):
                load(u, u, UNIT)
            sp.dma_start(WG[:, :, :], io["group"]).then_inc(group_in, 16)
            at = 4
            for u0, n, off in ((4, U_DNA - 4, 0), (U_DNA, N_DN, U_DNA), (U_K, U_DNB - U_K, N_DN),
                               (U_DNB, N_DN, U_DNB - N_DN), (U_RW, N_UNITS - U_RW, 2 * N_DN)):
                if n <= 0:
                    continue
                offset[0] = off
                w = DN_TILES * P if n == N_DN else UNIT
                with sp.Fori(0, n // 4) as i:
                    for j in range(4):
                        load(i * 4 + (u0 + j), (u0 + j) % 4, w)
                for j in range(n - n % 4, n):
                    load(u0 + j, (u0 + j) % 4, w)
            for j in range(4):
                sp.wait_ge(out_ready, j + 1)
                sp.dma_start(out[:, 2 * j:2 * j + 2, :], X[:, 2 * j:2 * j + 2, :]).then_inc(stored, 16)
            sp.wait_ge(stored, 64)

        @block.tensor
        def _(pe):
            def half_ready(u, half):
                pe.wait_ge(hi_ready, u * 2 + 1 + half)
                pe.wait_ge(lo_ready, u * 2 + 1 + half)

            def bank_free(g):
                if not isinstance(g, int) or g >= 2:
                    pe.wait_ge(evac_done, g - 1)

            def product(dst, wh, wl, xh, xl, first, last):
                nc.tensor.matmul(dst, wh, xh, start=first, stop=False, skip_group_check=True)
                nc.tensor.matmul(dst, wh, xl, start=False, stop=False, skip_group_check=True)
                return nc.tensor.matmul(dst, wl, xh, start=False, stop=last, skip_group_check=True)

            def channels(u, s, g, gp, rh, rl, k0=0, ready=None):
                slot = s % 2
                bank_free(g)
                for m in range(2):
                    half_ready(u, m)
                    for k in range(KD):
                        if ready is not None and m == 0:
                            ready(k)
                        c = slice((m * KD + k) * P, (m * KD + k + 1) * P)
                        last = product(PROJ[gp][:, m * T:(m + 1) * T], hi[:, slot, c], lo[:, slot, c],
                                       rh[:, k0 + k, :], rl[:, k0 + k, :], m == 0 and k == 0, k == KD - 1)
                last.then_inc(unit_done, 1)

            def tokens(u, s, g, gp, rh, rl, k0=0):
                slot = s % 2
                bank_free(g)
                half_ready(u, 1)
                for i in range(2):
                    for k in range(KD):
                        xh, xl = (r[:, k0 + k, i * P:(i + 1) * P] for r in (rh, rl))
                        wh, wl = (w[:, slot, k * T:(k + 1) * T] for w in (hi, lo))
                        dst = PROJ[gp][:, i * T:(i + 1) * T]
                        nc.tensor.matmul(dst, xh, wh, start=(i == 0 and k == 0), stop=False, skip_group_check=True)
                        nc.tensor.matmul(dst, xh, wl, start=False, stop=False, skip_group_check=True)
                        last = nc.tensor.matmul(dst, xl, wh, start=False, stop=(k == KD - 1), skip_group_check=True)
                last.then_inc(unit_done, 1)

            def from_x(base):
                def ready(k):
                    pe.wait_ge(xh_ready, base + k + 1)
                    pe.wait_ge(xl_ready, base + k + 1)
                return ready

            def from_e(base):
                def ready(k):
                    pe.wait_ge(eh_ready, base + k + 1)
                    pe.wait_ge(el_ready, base + k + 1)
                return ready

            def stats(n, cols):
                pe.wait_ge(sq_done, 8 * (n + 1))
                need(pe, rv_done, n)
                nc.tensor.matmul(STAT[:, 0:T], ones[:, :], ACC[:, 0, :], start=True, stop=False, skip_group_check=True)
                last = nc.tensor.matmul(STAT[:, 0:T], ones[:, :], ACC[:, 1, :], start=False, stop=True, skip_group_check=True)
                if cols:
                    for i in range(2):
                        for b in range(2):
                            last = nc.tensor.matmul(STAT[:, T + i:T + i + 1], ACC[:, b, i * P:(i + 1) * P], ones[:, 0:1],
                                                    start=False, stop=(b == 1), skip_group_check=True)
                last.then_inc(stat_done, 1)

            def simple(rh, rl, k0, ready, kind=channels):
                def unit(u):
                    g = first_group(u)
                    if kind is channels:
                        channels(u, u % 4, g, g % 2, rh, rl, k0, ready(u))
                    else:
                        tokens(u, u % 4, g, g % 2, rh, rl, k0)
                return unit

            def unit_out(u):
                if u in (U_OUTA, U_OUTB):
                    base = 0 if u == U_OUTA else 8
                    pe.wait_ge(mh_ready, base + 8)
                    pe.wait_ge(ml_ready, base + 8)
                simple(HH, HL, 0, lambda u: None)(u)

            def gu(u0):
                layer = 0 if u0 == U_GUA else 1
                for k in range(KD):
                    from_x(8 + 16 * layer)(k) if k == KD - 1 else None
                g0 = first_group(u0)
                channels(u0, u0 % 4, g0, g0 % 2, XH, XL)
                stats(2 + 2 * layer, False)
                over_units(pe, u0 + 1, N_GU - 1, lambda u, s: channels(
                    u, s, u + (g0 - u0), (g0 + (s - u0)) % 2, XH, XL))

            def down(u0):
                layer = 0 if u0 == U_DNA else 1
                g0 = first_group(u0)

                def half(u, s):
                    h = (s - u0) % 2
                    turn = ((s - u0) % 4) // 2
                    if h == 0:
                        g = (u - u0) // 2 + g0 if isinstance(u, int) else None
                        if g is not None:
                            bank_free(g)
                        else:
                            pe.wait_ge(evac_done, half_i[0] * 2 + (g0 + turn - 1))
                    for k in range(DN_TILES):
                        if k == 0:
                            half_ready(u, 0)
                        if k == 6:
                            half_ready(u, 1)
                        c = slice(k * P, (k + 1) * P)
                        t = h * DN_TILES + k
                        last = product(PROJ[(g0 + turn) % 2][:, 0:T], hi[:, s % 2, c], lo[:, s % 2, c],
                                       HH[:, t, :], HL[:, t, :], h == 0 and k == 0, h == 1 and k == DN_TILES - 1)
                    last.then_inc(unit_done, 1)

                pe.wait_ge(hh_ready, N_GU * (layer + 1))
                pe.wait_ge(hl_ready, N_GU * (layer + 1))
                half_i = [None]
                with pe.Fori(0, N_DN // 4) as i:
                    half_i[0] = i
                    for j in range(4):
                        half(i * 4 + (u0 + j), (u0 + j) % 4)

            def first_k(u):
                return from_x(16) if u == U_K else None

            def operands(g):
                layer, h = divmod(g, 4)
                q = HALF * (h % 2)
                return (QM[q:q + HALF, h // 2, :], MK[q:q + HALF, layer, h // 2, :],
                        lambda sj: MV[:, layer, sj, h * HALF:(h + 1) * HALF], q)

            def logits(g):
                Q, K, _, _ = operands(g)
                pe.wait_ge(evac_done, first_group(U_IN if g < 4 else M_UNITS[0]) + 1)
                need(pe, att_exp, g - 1)
                for i in range(2):
                    last = nc.tensor.matmul(LOG[g % 2][:, i * T:(i + 1) * T], Q[:, i * P:(i + 1) * P], K,
                                            start=(i == 0), stop=True, skip_group_check=True)
                last.then_inc(att_logits, 1)

            def turn(g):
                pe.wait_ge(att_norm, g + 1)
                need(pe, att_copied, g)
                for i in range(2):
                    for sj in range(2):
                        last = nc.tensor.transpose(TRA[:, sj * T + i * P:sj * T + (i + 1) * P],
                                                   PR[:, g % 2, i, sj * P:(sj + 1) * P], ident[:, :])
                last.then_inc(att_turned, 1)

            def pv(g):
                _, _, values, q = operands(g)
                pe.wait_ge(att_copied, g + 1)
                bank = OUTP[(g // 2) % 2]
                need(pe, att_out, g // 2 - 1)
                need(pe, sb_out, 0 if g < 4 else NSB // 2)
                for sj in range(2):
                    last = nc.tensor.matmul(bank[q:q + HALF, 0:T], values(sj), PTS[:, g % 2, sj, :],
                                            start=(sj == 0), stop=(sj == 1), skip_group_check=True)
                last.then_inc(att_pv, 1)

            def grouped():
                pe.wait_ge(group_in, 16)
                pe.wait_ge(pooled_done, 1)
                src = {0: SA, 1: SB, 2: SA, 3: SB}

                def piece(bank, col, p0, p1, g, d0, d1):
                    for n in range(2):
                        last = nc.tensor.matmul(bank[p0:p1, col:col + T], WG[:, 2 * g + n, d0:d1],
                                                src[g][:, 3 * g // 2 + n, 16:16 + T], start=(n == 0 and col == 0),
                                                stop=(n == 1), skip_group_check=True)
                    return last
                pe.wait_ge(att_exp, 4)
                pe.wait_ge(att_copied, 4)
                for b, bank in enumerate((LOG[0], LOG[1], TRA)):
                    for half in range(2):
                        t = 2 * b + half
                        col = half * T
                        g = (2 * t) // 3
                        if t % 3 == 0:
                            last = piece(bank, col, 0, P, g, 0, P)
                        elif t % 3 == 1:
                            piece(bank, col, 0, HALF, g, P, 192)
                            last = piece(bank, col, HALF, P, g + 1, 0, HALF)
                        else:
                            last = piece(bank, col, 0, P, g, HALF, 192)
                    last.then_inc(grouped_done, 1)

            def sbz(h):
                q = HALF * (h % 2)
                pe.wait_ge(evac_done, first_group(max(Q_UNITS[h // 4], K_UNITS[h // 4])) + 1)
                need(pe, sb_arg, h - 1)
                if h < 2:
                    pe.wait_ge(grouped_free, 3)
                Q, K = QT[q:q + HALF, h // 2, :], KT[q:q + HALF, h // 2, :]
                nc.tensor.matmul(LOG[h % 2][:, 0:P], K[:, P:T], Q[:, P:T], start=True, stop=False, skip_group_check=True)
                nc.tensor.matmul(LOG[h % 2][:, P:3 * P], K[:, 0:P], Q, start=False, stop=False,
                                 skip_group_check=True).then_inc(sb_z, 1)

            def sbcum(h):
                pe.wait_ge(sb_sp, h + 1)
                z, s = LOG[h % 2], SP[:, h % 2, :]
                nc.tensor.matmul(z[:, 0:P], ntri[:, :], s[:, 0:P], start=False, stop=False, skip_group_check=True)
                nc.tensor.matmul(z[:, P:3 * P], ntri[:, :], s[:, P:3 * P], start=False, stop=False, skip_group_check=True)
                nc.tensor.matmul(z[:, 2 * P:3 * P], nones[:, :], s[:, 0:P], start=False, stop=True,
                                 skip_group_check=True).then_inc(sb_cum, 1)

            def sbpv(h):
                q = HALF * (h % 2)
                pe.wait_ge(sb_wt, h + 1)
                pe.wait_ge(evac_done, first_group(V_UNITS[h // 4]) + 1)
                bank = OUTP[(h // 2) % 2]
                need(pe, sb_out, h // 2 - 1)
                if h < 4:
                    pe.wait_ge(att_out, 2)
                W, c = WT[:, h % 2, :], slice(h * HALF, (h + 1) * HALF)
                nc.tensor.matmul(bank[q:q + HALF, 0:T], V[:, 0, c], W[:, P:3 * P], start=True, stop=False,
                                 skip_group_check=True)
                nc.tensor.matmul(bank[q:q + HALF, P:T], V[:, 1, c], W[:, 0:P], start=False, stop=True,
                                 skip_group_check=True).then_inc(sb_pv, 1)

            def consts():
                pe.wait_ge(const_done, 1)

            def table_():
                pe.wait_ge(table_in, 1)
                for h in range(8):
                    bank = (LOG[0], LOG[1], TRA, OUTP[1])[h // 2]
                    last = nc.tensor.matmul(bank[:, (h % 2) * T:(h % 2 + 1) * T], RBX[:, h, :], OH, start=(h % 2 == 0),
                                            stop=True, skip_group_check=True)
                last.then_inc(table_done, 1)

            fills = turns()

            def claim(b):
                need(pe, taken[b], fills[b])
                fills[b] += 1

            def holds(b):
                need(pe, taken[b], fills[b])

            def mm(dst, w, x, first=False, last=True):
                return nc.tensor.matmul(dst, w, x, start=first, stop=last, skip_group_check=True)

            def unit_rw(u):
                simple(XH, XL, 0, lambda u: from_x(32) if u == U_RW else None)(u)

            def rw_first():
                unit_rw(U_RW)
                unit_rw(U_RW + 1)
                stats(6, True)

            def unit_lr(u):
                g = first_group(u)
                bank_free(g)
                half_ready(u, 0)
                half_ready(u, 1)
                for k in range(KD):
                    c = slice(k * P, (k + 1) * P)
                    last = product(PROJ[g % 2][:, 0:T], hi[:, u % 2, c], lo[:, u % 2, c], XH[:, k, :], XL[:, k, :],
                                   k == 0, k == KD - 1)
                last.then_inc(unit_done, 1)

            def low():
                pe.wait_ge(tanh_done, 1)
                pe.wait_ge(low_in, 16)
                for p0, banks in ((0, (LOG0, LOG1)), (HALF, (OUT0, OUT1))):
                    for n, b in enumerate(banks):
                        claim(b)
                        for j in range(2):
                            ct = 2 * n + j
                            last = mm(ps[b][:, j * T:(j + 1) * T], low_up[p0:p0 + HALF, ct * P:(ct + 1) * P],
                                      C[p0:p0 + HALF, 16, 1:], j == 0)
                        last.then_inc(filled[b], 1)

            def head_sums(src):
                for n, b in enumerate((LOG0, LOG1)):
                    claim(b)
                    for j in range(2):
                        last = mm(ps[b][:, j * T:(j + 1) * T], mask("heads")[:, 0, :], src[:, 2 * n + j, :], j == 0)
                    last.then_inc(filled[b], 1)

            def kk():
                pe.wait_ge(masks_in, 16)
                pe.wait_ge(kk_sq, 1)
                head_sums(TMP)

            def bonus():
                pe.wait_ge(bon_in, 1)
                head_sums(TMP)

            def mlog(h):
                q = HALF * (h % 2)
                b = (LOG0, LOG1)[h % 2]
                pe.wait_ge(evac_done, first_group(U_KA + 1) + 1)
                claim(b)
                for i in range(2):
                    last = mm(ps[b][:, i * T:(i + 1) * T], QA[q:q + HALF, h // 2, i * P:(i + 1) * P],
                              KA[q:q + HALF, h // 2, :], i == 0)
                last.then_inc(filled[b], 1)

            def mturn(h):
                pe.wait_ge(own_norm, h + 1)
                claim(TR)
                for i in range(2):
                    for sj in range(2):
                        last = nc.tensor.transpose(TRA[:, sj * T + i * P:sj * T + (i + 1) * P],
                                                   PR[:, h % 2, i, sj * P:(sj + 1) * P], ident[:, :])
                last.then_inc(filled[TR], 1)

            def mpv(h):
                q = HALF * (h % 2)
                b = (OUT0, OUT1)[(h // 2) % 2]
                holds(TR)
                pe.wait_ge(evac_done, first_group(U_VA + 1) + 1)
                if h % 2 == 0:
                    claim(b)
                else:
                    fills[b] += 1
                for sj in range(2):
                    last = mm(ps[b][q:q + HALF, 0:T], VA[:, sj, h * HALF:(h + 1) * HALF], PTS[:, h % 2, sj, :],
                              sj == 0, sj == 1)
                last.then_inc(filled[b], 1)

            def tok(ct):
                if ct == 0:
                    pe.wait_ge(hats_done, 1)
                for b, srcs in ((TR, ((KK, ct, 0), (AI, ct, 0))), (OUT0, ((C, 4 + ct, 1), (C, 8 + ct, 1)))):
                    claim(b)
                    for n, (src, t, off) in enumerate(srcs):
                        for i in range(2):
                            last = nc.tensor.transpose(ps[b][:, (2 * n + i) * P:(2 * n + i + 1) * P],
                                                       src[:, t, off + i * P:off + (i + 1) * P], ident[:, :])
                    last.then_inc(filled[b], 1)

            def grams(ct):
                for hh in range(2):
                    q = slice(HALF * hh, HALF * hh + HALF)

                    def at(src, t, off, i):
                        return src[q, t, off + i * P:off + (i + 1) * P]
                    a, b_, k, r = (KK, ct, 0), (AI, ct, 0), (C, 4 + ct, 1), (C, ct, 1)
                    for b, pairs in (((LOG0, LOG1)[hh], ((a, b_), (b_, a))), ((OUT0, OUT1)[hh], ((k, a), (b_, r))),
                                     ((TR, ST)[hh], ((k, r),))):
                        claim(b)
                        for n, (w, x) in enumerate(pairs):
                            for i in range(2):
                                last = mm(ps[b][:, (2 * n + i) * P:(2 * n + i + 1) * P], at(*w, i), at(*x, i),
                                          n == 0 and i == 0)
                        last.then_inc(filled[b], 1)

            def each(b, f):
                claim(b)
                for hh in range(2):
                    for i in range(2):
                        last = f(hh, i, 2 * hh + i)
                last.then_inc(filled[b], 1)

            def lv(ct):
                holds(OUT0)
                holds(OUT1)
                holds(TR)
                each(ST, lambda hh, i, n: mm(ps[ST][:, n * HALF:(n + 1) * HALF], LK[:, hh, i, :],
                                             TOK[:, 2, i, hh * HALF:(hh + 1) * HALF], n == 0))

            def level(ct, lvl):
                for hh, b in ((0, LOG0), (1, LOG1)):
                    if lvl == 0:
                        pe.wait_ge(inverse_done, 2 * ct + hh + 1)
                    holds((OUT0, OUT1)[hh])
                    claim(b)
                    for i in range(2):
                        last = mm(ps[b][:, i * P:(i + 1) * P], AM[:, hh, i, :], NN[:, hh, i, :], i == 0)
                    last.then_inc(filled[b], 1)
                for hh, b in ((0, OUT0), (1, OUT1)):
                    holds((LOG0, LOG1)[hh])
                    claim(b)
                    for i in range(2):
                        last = mm(ps[b][:, i * P:(i + 1) * P], MM[:, hh, i, :], YM[:, hh, i, :], i == 0)
                    if lvl < 4:
                        for i in range(2):
                            last = mm(ps[b][:, T + i * P:T + (i + 1) * P], YM[:, hh, i, :], MM[:, hh, i, :])
                    last.then_inc(filled[b], 1)

            def apply(ct):
                holds(OUT0)
                holds(OUT1)
                holds(ST)
                each(LOG0, lambda hh, i, n: mm(ps[LOG0][:, n * P:(n + 1) * P], NN[:, hh, i, :], RHS[:, hh, i, :], n == 0))
                each(TR, lambda hh, i, n: mm(ps[TR][hh * HALF:(hh + 1) * HALF, i * P:(i + 1) * P],
                                             RHS[:, hh, i, 0:HALF], NN[:, hh, i, :], i == 0))

            def chunks(ct):
                holds(LOG0)
                holds(TR)
                claim(LOG1)
                claim(OUT0)
                for c in range(3):
                    i, r = c // 2, slice(CHUNK * (c % 2), CHUNK * (c % 2) + CHUNK)
                    b, col = ((LOG1, 0), (OUT0, 0), (LOG1, P))[c]
                    for hh in range(2):
                        o, ch = slice(hh * HALF, (hh + 1) * HALF), slice(hh * HALF, (hh + 1) * HALF)
                        mm(ps[b][o, col:col + HALF], AM[r, hh, i, 0:HALF], TOK[r, 0, i, ch], col == 0)
                        mm(ps[b][o, col + HALF:col + P], TOK[r, 0, i, ch], AM[r, hh, i, HALF:P], False, False)
                        last = mm(ps[b][o, col + HALF:col + P], TOK[r, 1, i, ch], TOK[r, 2, i, ch])
                    if c:
                        last.then_inc(filled[b], 1)

            def scan(ct, c):
                pe.wait_ge(state_done, 4 * ct + c)
                if c == 1:
                    return
                claim(LOG0)
                for hh in range(2):
                    o = slice(hh * HALF, (hh + 1) * HALF)
                    last = mm(ps[LOG0][o, 0:HALF], GT[o, c - 1, 0, :], TTB[o, c - 1, o], True)
                last.then_inc(filled[LOG0], 1)

            def sa(ct):
                pe.wait_ge(state_done, 4 * ct + 4)
                for hh, b in ((0, OUT1), (1, ST)):
                    o = slice(hh * HALF, (hh + 1) * HALF)
                    claim(b)
                    for c in range(4):
                        i, p0 = c // 2, CHUNK * (c % 2)
                        last = mm(ps[b][p0:p0 + CHUNK, i * HALF:(i + 1) * HALF], MAT[o, c * CHUNK:(c + 1) * CHUNK],
                                  TTB[o, c, o], c < 2)
                    last.then_inc(filled[b], 1)

            def yt(ct):
                claim(LOG1)
                for c in range(4):
                    mm(ps[LOG1][:, c * CHUNK:(c + 1) * CHUNK], TTB[:, c, :], C[:, ct, 1 + c * CHUNK:1 + (c + 1) * CHUNK],
                       c == 0, False)
                holds(OUT1)
                holds(ST)
                for hh in range(2):
                    o = slice(hh * HALF, (hh + 1) * HALF)
                    for i in range(2):
                        mm(ps[LOG1][o, i * P:(i + 1) * P], SAO[:, hh, i, :], MB[:, hh, i, :], False, False)
                        last = mm(ps[LOG1][o, i * P:(i + 1) * P], TOK[:, 2, i, o], MC[:, hh, i, :])
                last.then_inc(filled[LOG1], 1)

            def gn(ct):
                pe.wait_ge(y_out, ct + 1)
                claim(TR)
                mm(ps[TR][:, 0:T], mask("heads")[:, 0, :], KK[:, ct, :], True).then_inc(filled[TR], 1)

            def gn2(ct):
                pe.wait_ge(gn_sq, ct + 1)
                claim(TR)
                mm(ps[TR][:, 0:T], mask("heads")[:, 0, :], YQ[:, :], True).then_inc(filled[TR], 1)

            def unit_pab(u):
                g = first_group(u)
                if u == U_PAB:
                    for s_, n in ((yah_ready, 4), (yal_ready, 4), (ybh_ready, 4), (ybl_ready, 4)):
                        pe.wait_ge(s_, n)
                half_ready(u, 0)
                half_ready(u, 1)
                for which, (rh, rl) in enumerate(((YAH, YAL), (YBH, YBL))):
                    bank_free(g + which)
                    for m in range(2):
                        for k in range(4):
                            c = slice((m * KD + 4 * which + k) * P, (m * KD + 4 * which + k + 1) * P)
                            last = product(PROJ[(g + which) % 2][:, m * T:(m + 1) * T], hi[:, u % 2, c], lo[:, u % 2, c],
                                           rh[:, k, :], rl[:, k, :], m == 0 and k == 0, k == 3)
                last.then_inc(unit_done, 1)

            def unit_out2(u):
                simple(XH, XL, 0, lambda u: from_x(40) if u == U_OUT2 else None)(u)

            def unit_eup(u):
                g = first_group(u)
                pe.wait_ge(pl_ready, 2)
                pe.wait_ge(ph_ready, 2)
                half_ready(u, 0)
                half_ready(u, 1)
                for j in range(4):
                    bank_free(g + j)
                    for m in range(2):
                        for k in range(2):
                            n = (2 * j + m) * 2 + k
                            last = product(PROJ[(g + j) % 2][:, m * T:(m + 1) * T], hi[:, u % 2, n * P:(n + 1) * P],
                                           lo[:, u % 2, n * P:(n + 1) * P], PH[:, k, :], PL[:, k, :],
                                           m == 0 and k == 0, k == 1)
                    if j < 3:
                        last.then_inc(e_part, 1)
                last.then_inc(unit_done, 1)

            def unit_egate(u):
                simple(XH, XL, 0, lambda u: from_x(48) if u == U_EGATE else None)(u)

            run({
                "consts": consts, "table": table_,
                "norm_mem": lambda: None,
                "unit_mk": lambda u: (simple(HH, HL, 8, lambda u: from_e(0) if u == 0 else None)(u),
                                      stats(0, True) if u == 0 else None),
                "unit_mv": simple(HH, HL, 8, None, tokens),
                "stats": lambda n, c: stats(n, c),
                "unit_qm": lambda u: simple(XH if u < U_GUA else HH, XL if u < U_GUA else HL, 0 if u < U_GUA else 8,
                                            lambda u: from_x(0) if u == U_IN else None)(u),
                "unit_pool": simple(XH, XL, 0, lambda u: None),
                "unit_out": unit_out,
                "gu": gu, "down": down,
                "unit_k": simple(XH, XL, 0, first_k),
                "unit_q": simple(HH, HL, 8, lambda u: from_e(8) if u == min(Q_UNITS + M_UNITS) else None),
                "unit_v": simple(XH, XL, 0, None, tokens),
                "logits": logits, "turn": turn, "pv": pv, "grouped": grouped,
                "sbz": sbz, "sbcum": sbcum, "sbpv": sbpv,
                "rw_first": rw_first, "unit_rw": unit_rw, "unit_lr": unit_lr, "low": low, "kk": kk, "bonus": bonus,
                "unit_qa": unit_rw, "unit_ka": unit_rw, "unit_va": simple(XH, XL, 0, None, tokens), "unit_za": unit_rw,
                "unit_gate": unit_rw, "mlog": mlog, "mturn": mturn, "mpv": mpv, "tok": tok, "grams": grams, "lv": lv,
                "level": level, "apply": apply, "chunks": chunks, "scan": scan, "sa": sa, "yt": yt, "gn": gn, "gn2": gn2,
                "unit_pab": unit_pab, "unit_out2": unit_out2, "unit_eup": unit_eup, "unit_egate": unit_egate,
            })

        @block.scalar
        def _(act):
            def split_hi(u, s, n):
                if isinstance(u, int):
                    act.wait_ge(loaded[s], 16 * (u // 4 + 1))
                    need(act, unit_done, u - 1)
                else:
                    act.wait_ge(loaded[s], arrivals(u, s))
                    act.wait_ge(unit_done, u - 1)
                h = n // 2 if n == UNIT else 6 * P
                nc.scalar.activation(hi[:, s % 2, 0:h], raw[:, s, 0:h], ACT.Copy).then_inc(hi_ready, 1)
                nc.scalar.activation(hi[:, s % 2, h:n], raw[:, s, h:n], ACT.Copy).then_inc(hi_ready, 1)

            arrivals_at = {}

            def arrivals(u, s):
                i, base = arrivals_at["now"]
                return i * 16 + 16 * ((base[s]) // 4 + 1)

            def loop_units(u0, n, body):
                if n >= 8:
                    with act.Fori(0, n // 4) as i:
                        for j in range(4):
                            ahead = u0 + j + 2
                            arrivals_at["now"] = (i, {ahead % 4: ahead})
                            body(i * 4 + (u0 + j), (u0 + j) % 4)
                    n0 = n - n % 4
                else:
                    n0 = 0
                for j in range(n0, n):
                    body(u0 + j, (u0 + j) % 4)

            def ahead(u):
                if u + 2 < N_UNITS:
                    split_hi(u + 2, (u + 2) % 4, width(u + 2))

            def split_tile(dst, src, gain, ready):
                kw = {"scale": gain} if gain is not None else {}
                nc.scalar.activation(dst, src, ACT.Copy, **kw).then_inc(ready, 1)

            def rstd(n, cols):
                act.wait_ge(rv_done, n + 1)
                nc.scalar.activation(RS[:, n % 2, 0, :], RV[:, 0:T], ACT.Sqrt)
                last = nc.scalar.activation(RS[:, n % 2, 1, :], RV[:, 0:T], ACT.Sqrt)
                if cols:
                    last = nc.scalar.activation(RSC[:, n % 2, :], RV[:, T:T + 2], ACT.Sqrt)
                last.then_inc(rs_done, 1)

            def mem_in_():
                act.wait_ge(vecs_in, 16)
                act.wait_ge(mem_in, 16)
                for k in range(KD):
                    split_tile(HH[:, 8 + k, :], MEM[:, k, :], vec[:, VEC["mem_norm"] + k:VEC["mem_norm"] + k + 1], eh_ready)

            def x_in_():
                act.wait_ge(x_in, 16)
                for k in range(KD):
                    split_tile(XH[:, k, :], X[:, k, :], vec[:, VEC["a_norm_mix"] + k:VEC["a_norm_mix"] + k + 1], xh_ready)

            def unit_out(u):
                ahead(u)
                layer = 0 if u < U_GUA else 1
                j = u - (U_OUTA, U_OUTB)[layer]
                gain = VEC[("a_norm_ffn", "b_norm_ffn")[layer]]
                for m in (2 * j, 2 * j + 1):
                    act.wait_ge(x_done, 16 * layer + m + 1)
                    split_tile(XH[:, m, :], X[:, m, :], vec[:, gain + m:gain + m + 1], xh_ready)

            def gu(u0):
                layer = 0 if u0 == U_GUA else 1
                m0 = N_GU * layer

                def step(u, s, n):
                    split_hi(u + 2, (s + 2) % 4, n)
                    hidden(u, s)

                def hidden(u, s):
                    g = s % 2
                    act.wait_ge(gate_in, u + (1 + m0 - u0))
                    nc.scalar.activation(SG[:, g, :], GU[:, g, 0, :], ACT.Silu).then_inc(silu_done, 1)
                    act.wait_ge(h_done, u + (1 + m0 - u0))
                    m = u - u0
                    dst = HH[:, m, :] if isinstance(m, int) else HH[:, bass.ds(m, 1), :]
                    src = GU[:, g, 1, :] if isinstance(m, int) else GU[:, g, 1:2, :]
                    nc.scalar.activation(dst, src, ACT.Copy).then_inc(hh_ready, 1)

                split_hi(u0 + 2, (u0 + 2) % 4, UNIT)
                rstd(2 + 2 * layer, False)
                hidden(u0, u0 % 4)
                loop_units(u0 + 1, N_GU - 6, lambda u, s: step(u, s, UNIT))
                for u in range(u0 + N_GU - 5, u0 + N_GU):
                    step(u, u % 4, width(u + 2))

            def down(u0):
                layer = 0 if u0 == U_DNA else 1

                def half(u, s, n, m):
                    if n:
                        split_hi(u + 2, (s + 2) % 4, n)
                    if (s - u0) % 2 == 1:
                        act.wait_ge(x_done, m + (8 + 16 * layer + 1))
                        if isinstance(m, int):
                            dst, src, gain = XH[:, m, :], X[:, m, :], gains[:, m:m + 1]
                        else:
                            dst, src, gain = (a[:, bass.ds(m, 1)] if a is gains else a[:, bass.ds(m, 1), :]
                                              for a in (XH, X, gains))
                        nc.scalar.activation(dst, src, ACT.Copy, scale=gain).then_inc(xh_ready, 1)

                c = VEC["kv_norm"]
                gains = vec[:, c:c + KD] if layer == 0 else gfp[:, :]
                with act.Fori(0, N_DN // 4 - 1) as i:
                    for j in range(4):
                        ahead_u = u0 + j + 2
                        arrivals_at["now"] = (i, {ahead_u % 4: ahead_u})
                        half(i * 4 + (u0 + j), (u0 + j) % 4, DN_TILES * P, i * 2 + j // 2)
                for j in range(N_DN - 4, N_DN):
                    u = u0 + j
                    half(u, u % 4, width(u + 2) if u + 2 < N_UNITS else 0, j // 2)

            def esplit(part):
                c = VEC["b_norm_mix"]
                act.wait_ge(unit_done, U_K)
                for k in range(4 * part, 4 * part + 4):
                    split_tile(HH[:, 8 + k, :], X[:, k, :], vec[:, c + k:c + k + 1], eh_ready)

            def soft(g):
                act.wait_ge(att_max, g + 1)
                need(act, att_turned, g - 1)
                for i in range(2):
                    last = nc.scalar.activation(PR[:, g % 2, i, :], LOG[g % 2][:, i * T:(i + 1) * T], ACT.Exp,
                                                bias=NM[:, g % 2, i:i + 1], accum_out=SM[:, g % 2, i:i + 1])
                last.then_inc(att_exp, 1)

            def turn(g):
                act.wait_ge(att_turned, g + 1)
                need(act, att_pv, g - 1)
                nc.scalar.activation(PTS[:, g % 2, :, :], TRA[:, :].rearrange("p (a b) -> p a b", a=2),
                                     ACT.Copy).then_inc(att_copied, 1)

            def pv(g):
                if g % 2:
                    act.wait_ge(att_pv, g + 1)
                    t = SBT + (g % 4) // 2
                    nc.scalar.activation(HH[:, t, :], OUTP[(g // 2) % 2][:, 0:T], ACT.Copy).then_inc(mh_ready, 1)

            def grouped():
                for t in range(6):
                    act.wait_ge(grouped_done, t // 2 + 1)
                    bank = (LOG[0], LOG[1], TRA)[t // 2]
                    c = VEC["a_scale"] + t
                    nc.scalar.activation(HH[:, t, :], bank[:, (t % 2) * T:(t % 2 + 1) * T], ACT.Copy,
                                         scale=vec[:, c:c + 1]).then_inc(mh_ready, 1)

            def log_table():
                nc.scalar.preload_act_table_set("natural_log_exp_and_others")

            def sbz(h):
                act.wait_ge(sb_z, h + 1)
                L = LG[:, h % 2, :]
                need(act, sb_sp, h - 1)
                nc.scalar.activation(L, LOG[h % 2][:, 0:3 * P], ACT.Abs).then_inc(sb_abs, 1)
                act.wait_ge(sb_abs, h + 1)
                nc.scalar.activation(L, L, ACT.Exp, scale=-1.0).then_inc(sb_exp, 1)
                act.wait_ge(sb_exp, h + 1)
                nc.scalar.activation(L, L, ACT.Ln, bias=1.0).then_inc(sb_ln, 1)

            def sbcum(h):
                act.wait_ge(sb_arg, h + 1)
                need(act, sb_pv, h - 1)
                nc.scalar.activation(WT[:, h % 2, :], SP[:, h % 2, :], ACT.Exp).then_inc(sb_wt, 1)

            def sbpv(h):
                if h % 2:
                    act.wait_ge(sb_pv, h + 1)
                    nc.scalar.activation(HH[:, h // 2, :], OUTP[(h // 2) % 2][:, 0:T], ACT.Copy).then_inc(mh_ready, 1)

            fills = turns()

            def full(b):
                fills[b] += 1
                act.wait_ge(filled[b], fills[b])

            def skip(*banks):
                for b in banks:
                    fills[b] += 1

            def rw_first():
                ahead(U_RW)
                ahead(U_RW + 1)
                rstd(6, True)

            def low():
                act.wait_ge(shifted, 5)
                nc.scalar.activation(C[0:HALF, 16, 1:], C[0:HALF, 16, 1:], ACT.Tanh).then_inc(tanh_done, 1)
                for dst, bias, banks in ((SW, "w0_2", (LOG0, LOG1)), (AI, "a0_2", (OUT0, OUT1))):
                    for n, b in enumerate(banks):
                        full(b)
                        for j in range(2):
                            c = VEC[bias] + 2 * n + j
                            last = nc.scalar.activation(dst[:, 2 * n + j, :], ps[b][:, j * T:(j + 1) * T], ACT.Sigmoid,
                                                        bias=vec[:, c:c + 1])
                        last.then_inc(taken[b], 1)
                act.wait_ge(shifted, 4)
                nc.scalar.activation(C[:, 12:16, 1:], C[:, 12:16, 1:], ACT.Silu).then_inc(z_done, 1)

            def kk():
                skip(LOG0, LOG1)
                act.wait_ge(kk_rv, 1)
                nc.scalar.activation(TMP[:, :, :], TMP[:, :, :], ACT.Sqrt).then_inc(kk_rn, 1)

            def bonus():
                skip(LOG0, LOG1)

            def exps():
                act.wait_ge(cum_done, 1)
                act.wait_ge(filled[LOG1], fills[LOG1])
                nc.scalar.activation(TMP[:, :, :], CUM[:, :, :], ACT.Exp, scale=-DECAY).then_inc(exp_done, 1)
                nc.scalar.activation(ED[:, :, :], CUM[:, :, CHUNK - 1::CHUNK], ACT.Exp, scale=-DECAY).then_inc(exp_done, 1)
                act.wait_ge(exp_done, 2)
                nc.scalar.activation(CUM[:, :, :], CUM[:, :, :], ACT.Exp, scale=DECAY).then_inc(exp_done, 1)
                nc.scalar.activation(SW[:, :, :], SW[:, :, :], ACT.Exp, scale=-DECAY).then_inc(exp_done, 1)

            def unit_za(u):
                ahead(u)
                j = u - U_ZA
                act.wait_ge(za_in, j + 1)
                z = ZA[:, 2 * j:2 * j + 2, :]
                nc.scalar.activation(z, z, ACT.Silu).then_inc(za_done, 1)

            def unit_gate(u):
                ahead(u)
                j = u - U_GATE
                act.wait_ge(gates_in, j + 1)
                z = SGT[:, 2 * j:2 * j + 2, :]
                nc.scalar.activation(z, z, ACT.Sigmoid).then_inc(gates_done, 1)

            def mlog(h):
                skip((LOG0, LOG1)[h % 2])

            def msoft(h):
                act.wait_ge(own_max, h + 1)
                for i in range(2):
                    last = nc.scalar.activation(PR[:, h % 2, i, :], PR[:, h % 2, i, :], ACT.Exp,
                                                bias=NM[:, h % 2, i:i + 1], accum_out=SM[:, h % 2, i:i + 1])
                last.then_inc(own_exp, 1)

            def mturn(h):
                if h >= 2:
                    b = (OUT0, OUT1)[((h - 2) // 2) % 2]
                    act.wait_ge(filled[b], pv_count[h - 2])
                full(TR)
                nc.scalar.activation(PTS[:, h % 2, :, :], TRA[:, :].rearrange("p (a b) -> p a b", a=2),
                                     ACT.Copy).then_inc(taken[TR], 1)

            pv_count = {}

            def mpv(h):
                b = (OUT0, OUT1)[(h // 2) % 2]
                fills[b] += 1
                pv_count[h] = fills[b]
                if h % 2:
                    act.wait_ge(own_y, h // 2 + 1)
                    nc.scalar.activation(YAH[:, h // 2, :], ZA[:, h // 2, :], ACT.Copy).then_inc(yah_ready, 1)

            def tok(ct):
                full(TR)
                nc.scalar.activation(RHS[:, :, :, 0:HALF], TRA[:, 0:T].rearrange("p (i h c) -> p h i c", i=2, h=2), ACT.Copy)
                nc.scalar.activation(TOK[:, 0, :, :], TRA[:, T:2 * T].rearrange("p (a b) -> p a b", a=2),
                                     ACT.Copy).then_inc(taken[TR], 1)
                full(OUT0)
                nc.scalar.activation(TOK[:, 1:3, :, :], ps[OUT0][:, :].rearrange("p (k a b) -> p k a b", k=2, a=2),
                                     ACT.Copy).then_inc(taken[OUT0], 1)

            def grams(ct):
                skip(LOG0, LOG1, OUT0, OUT1, TR, ST)

            def lv(ct):
                full(ST)
                nc.scalar.activation(RHS[:, :, :, HALF:P], ps[ST][:, 0:T].rearrange("p (h i c) -> p h i c", h=2, i=2),
                                     ACT.Copy).then_inc(taken[ST], 1)

            def level(ct, lvl):
                skip(LOG0, LOG1, OUT0, OUT1)

            def apply(ct):
                full(LOG0)
                nc.scalar.activation(AM[:, :, :, :], ps[LOG0][:, :].rearrange("p (h i c) -> p h i c", h=2, i=2),
                                     ACT.Copy).then_inc(taken[LOG0], 1)
                full(TR)
                nc.scalar.activation(MAT[:, :], ps[TR][:, 0:T], ACT.Copy).then_inc(taken[TR], 1)

            def chunks(ct):
                full(LOG1)
                nc.scalar.activation(GT[:, 0:3:2, :, :], ps[LOG1][:, 0:T].rearrange("p (c g v) -> p c g v", c=2, g=2),
                                     ACT.Copy).then_inc(taken[LOG1], 1)
                full(OUT0)
                nc.scalar.activation(GT[:, 1, :, :], ps[OUT0][:, 0:P].rearrange("p (g v) -> p g v", g=2),
                                     ACT.Copy).then_inc(taken[OUT0], 1)

            def scan(ct, c):
                if c > 1:
                    skip(LOG0)

            def sa(ct):
                skip(OUT1, ST)

            def yt(ct):
                full(LOG1)
                nc.scalar.activation(KK[:, ct, :], ps[LOG1][:, 0:T], ACT.Copy).then_inc(taken[LOG1], 1)
                act.wait_ge(taken[LOG1], fills[LOG1])
                act.sem_inc(y_out, 1)

            def gn(ct):
                skip(TR)

            def gn2(ct):
                skip(TR)
                act.wait_ge(gn_rv, ct + 1)
                nc.scalar.activation(YQ[:, :], YQ[:, :], ACT.Sqrt).then_inc(gn_rs, 1)

            def gn3(ct):
                act.wait_ge(yb_done, ct + 1)
                if ct == 0:
                    act.wait_ge(yah_ready, 4)
                    act.wait_ge(taken[OUT1], 1)
                nc.scalar.activation(YBH[:, ct, :], KK[:, ct, :], ACT.Copy).then_inc(ybh_ready, 1)

            def unit_pab(u):
                ahead(u)
                j = u - U_PAB
                act.wait_ge(merged, j + 1)
                for m in (2 * j, 2 * j + 1):
                    split_tile(XH[:, m, :], SGT[:, m, :], None, xh_ready)

            def p_in_():
                act.wait_ge(p_in, 16)
                for k in range(2):
                    split_tile(PH[:, k, :], PIN[:, k, :], None, ph_ready)

            def post():
                for m in range(KD):
                    act.wait_ge(y_done, 8 + m + 1)
                    split_tile(XH[:, m, :], X[:, m, :], None, xh_ready)

            def unit_egate(u):
                ahead(u)
                j = u - U_EGATE
                act.wait_ge(unit_done, u + 1)
                need(act, out_ready, j - 1)
                bank = PROJ[first_group(u) % 2][:, :].rearrange("p (a b) -> p a b", a=2)
                nc.scalar.activation(SIG[:, j % 2, :, :], bank, ACT.Sigmoid).then_inc(sig_done, 1)

            run({
                "rw_first": rw_first, "unit_rw": ahead, "unit_lr": ahead, "low": low, "kk": kk, "bonus": bonus, "exps": exps,
                "unit_qa": ahead, "unit_ka": ahead, "unit_va": ahead, "unit_za": unit_za, "unit_gate": unit_gate,
                "mlog": mlog, "msoft": msoft, "mturn": mturn, "mpv": mpv, "tok": tok, "grams": grams, "lv": lv,
                "level": level, "apply": apply, "chunks": chunks, "scan": scan, "sa": sa, "yt": yt, "gn": gn, "gn2": gn2, "gn3": gn3,
                "unit_pab": unit_pab, "unit_out2": ahead, "unit_eup": ahead, "p_in": p_in_, "post": post,
                "unit_egate": unit_egate,
                "split": lambda u: split_hi(u, u % 4, UNIT),
                "mem_in": mem_in_, "x_in": x_in_,
                "unit_mk": lambda u: (rstd(0, True) if u == 0 else None, ahead(u)),
                "unit_mv": ahead, "stats": lambda n, c: rstd(n, c),
                "unit_qm": ahead, "unit_pool": ahead, "unit_out": unit_out, "gu": gu, "down": down,
                "unit_k": ahead, "unit_q": ahead, "unit_v": ahead, "esplit": esplit,
                "soft": soft, "turn": turn, "pv": pv, "grouped": grouped,
                "sbz": sbz, "sbcum": sbcum, "sbpv": sbpv, "log_table": log_table,
            })

        @block.vector
        def _(dve):
            chain = [0]

            def link(ins):
                chain[0] += 1
                ins.then_inc(dve_chain, 1)
                dve.wait_ge(dve_chain, chain[0])

            def split_lo(u, s, n):
                h = n // 2 if n == UNIT else 6 * P
                for half, (a, b) in enumerate(((0, h), (h, n))):
                    dve.wait_ge(hi_ready, u * 2 + 1 + half)
                    nc.vector.tensor_tensor(lo[:, s % 2, a:b], raw[:, s, a:b], hi[:, s % 2, a:b].bitcast(F32),
                                            ALU.subtract).then_inc(lo_ready, 1)

            def ahead(u):
                if u + 2 < N_UNITS:
                    split_lo(u + 2, (u + 2) % 4, width(u + 2))

            def bank_of(u):
                g = first_group(u)
                return PROJ[g % 2][:, :]

            def lower(dst, src, gain, upper):
                if gain is None:
                    return nc.vector.tensor_tensor(dst, src, upper.bitcast(F32), ALU.subtract)
                return nc.vector.scalar_tensor_tensor(dst, src, gain, upper.bitcast(F32), ALU.mult, ALU.subtract)

            def rstd(n, cols):
                w = T + 2 if cols else T
                dve.wait_ge(stat_done, n + 1)
                need(dve, rs_done, n)
                link(nc.vector.tensor_scalar(RV[:, 0:w], STAT[:, 0:w], 1.0 / D, EPS, ALU.mult, ALU.add))
                nc.vector.reciprocal(RV[:, 0:w], RV[:, 0:w]).then_inc(rv_done, 1)

            def scaled(u, dst, n, factor=None):
                dve.wait_ge(unit_done, u + 1)
                dve.wait_ge(rs_done, n + 1)
                src = bank_of(u).rearrange("p (a b) -> p a b", a=2)
                r = RS[:, n % 2, :, :]
                if factor is None:
                    nc.vector.tensor_tensor(dst, src, r, ALU.mult).then_inc(evac_done, 1)
                else:
                    nc.vector.scalar_tensor_tensor(dst, src, factor, r, ALU.mult, ALU.mult).then_inc(evac_done, 1)
                ahead(u)

            def mem_in_():
                for k in range(KD):
                    dve.wait_ge(eh_ready, k + 1)
                    c = VEC["mem_norm"] + k
                    lower(HL[:, 8 + k, :], MEM[:, k, :], vec[:, c:c + 1], HH[:, 8 + k, :]).then_inc(el_ready, 1)

            def x_in_():
                for k in range(KD):
                    dve.wait_ge(xh_ready, k + 1)
                    c = VEC["a_norm_mix"] + k
                    lower(XL[:, k, :], X[:, k, :], vec[:, c:c + 1], XH[:, k, :]).then_inc(xl_ready, 1)

            def pads():
                dve.wait_ge(table_stored, 64)
                nc.vector.memset(UP[:, :, 0:16], 0.0).then_inc(pads_done, 1)
                nc.vector.memset(SA[:, :, 0:16], 0.0).then_inc(pads_done, 1)
                nc.vector.memset(SB[:, :, 0:16], 0.0).then_inc(pads_done, 1)
                dve.wait_ge(const_done, 2)
                for g in range(4):
                    link(nc.vector.tensor_scalar(INV[:, g, :], INV[:, g, :], float(2 << g), None, ALU.min))
                nc.vector.reciprocal(INV[:, :, :], INV[:, :, :]).then_inc(inv_done, 1)
                dve.wait_ge(pads_done, 3)
                dve.wait_ge(inv_done, 1)
                a, b = VEC["final_norm"], VEC["g_pre_2"]
                link(nc.vector.tensor_tensor(gfp[:, :], vec[:, a:a + KD], vec[:, b:b + KD], ALU.mult))

            def unit_mk(u):
                if u == 0:
                    rstd(0, True)
                scaled(u, MK[:, 0 if u == 0 else 1, :, :], 0)

            def unit_mv(u):
                values(u, lambda i: MV[:, 0 if u == 1 else 1, i, :], 0)

            def values(u, dst, n):
                dve.wait_ge(unit_done, u + 1)
                for i in range(2):
                    last = nc.vector.tensor_scalar(dst(i), bank_of(u)[:, i * T:(i + 1) * T], RSC[:, n % 2, i:i + 1], None, ALU.mult)
                last.then_inc(evac_done, 1)
                ahead(u)

            def unit_qm(u):
                n = 1 if u < U_GUA else 3
                scaled(u, QM[:, :, :], n, SCALE)

            def unit_pool(u):
                j = u - U_IN - 1
                scaled(u, UP[:, 2 * j:2 * j + 2, 16:], 1)

            def pool():
                w = slice(16, 16 + T)

                def shifted(by):
                    return slice(16 - by, 16 - by + T)
                dve.wait_ge(evac_done, first_group(U_IN + 3) + 1)
                link(nc.vector.tensor_tensor(SA[:, :, w], UP[:, :, w], UP[:, :, shifted(1)], ALU.add))
                link(nc.vector.tensor_tensor(SB[:, 1:6, w], SA[:, 1:6, w], SA[:, 1:6, shifted(2)], ALU.add))
                link(nc.vector.tensor_tensor(SA[:, 3:6, w], SB[:, 3:6, w], SB[:, 3:6, shifted(4)], ALU.add))
                link(nc.vector.tensor_tensor(SB[:, 4:6, w], SA[:, 4:6, w], SA[:, 4:6, shifted(8)], ALU.add))
                parts = []
                for g, src in enumerate((SA, SB, SA, SB)):
                    t0 = 3 * g // 2
                    parts += [(src, g, t, a, b) for t, a, b in
                              ([(t0, 0, P), (t0 + 1, 0, HALF)] if g % 2 == 0 else [(t0, HALF, P), (t0 + 1, 0, P)])]
                for src, g, t, a, b in parts:
                    last = nc.vector.tensor_tensor(src[a:b, t, w], src[a:b, t, w], INV[a:b, g, :], ALU.mult)
                link(last)
                for src, g, t, a, b in parts:
                    last = nc.vector.tensor_tensor(src[a:b, t, w], src[a:b, t, w], UP[a:b, t, w], ALU.subtract)
                last.then_inc(pooled_done, 1)

            def grouped():
                for t in range(6):
                    dve.wait_ge(mh_ready, 2 + 2 * (t // 2) + 2)
                    bank = (LOG[0], LOG[1], TRA)[t // 2]
                    c = VEC["a_scale"] + t
                    last = lower(HL[:, t, :], bank[:, (t % 2) * T:(t % 2 + 1) * T], vec[:, c:c + 1], HH[:, t, :])
                    last.then_inc(ml_ready, 1)
                dve.wait_ge(ml_ready, 8)
                dve.sem_inc(grouped_free, 3)

            def unit_out(u):
                layer = 0 if u < U_GUA else 1
                j = u - (U_OUTA, U_OUTB)[layer]
                if layer == 0 and j == 0:
                    dve.wait_ge(x_in, 16)
                dve.wait_ge(unit_done, u + 1)
                src = bank_of(u).rearrange("p (a b) -> p a b", a=2)
                nc.vector.tensor_tensor(X[:, 2 * j, :], X[:, 2 * j, :], src[:, 0, :], ALU.add).then_inc(x_done, 1)
                nc.vector.tensor_tensor(X[:, 2 * j + 1, :], X[:, 2 * j + 1, :], src[:, 1, :], ALU.add).then_inc(x_done, 1)
                dve.wait_ge(x_done, 16 * layer + 2 * j + 2)
                dve.sem_inc(evac_done, 1)
                ahead(u)
                if j > 0:
                    xlower(layer, 2 * j - 2)

            def xlower(layer, m0):
                gain = VEC[("a_norm_ffn", "b_norm_ffn")[layer]]
                for m in (m0, m0 + 1):
                    dve.wait_ge(xh_ready, 8 + 16 * layer + m + 1)
                    lower(XL[:, m, :], X[:, m, :], vec[:, gain + m:gain + m + 1], XH[:, m, :]).then_inc(xl_ready, 1)

            def gu(u0):
                layer = 0 if u0 == U_GUA else 1
                m0 = N_GU * layer
                g0 = first_group(u0)

                def hidden_in(u, s):
                    dve.wait_ge(unit_done, u + 1)
                    src = PROJ[(g0 + (s - u0)) % 2][:, :].rearrange("p (a b) -> p a b", a=2)
                    nc.vector.tensor_tensor(GU[:, s % 2, :, :], src, RS[:, 0, :, :],
                                            ALU.mult).then_inc(gate_in, 1)
                    dve.wait_ge(gate_in, u + (1 + m0 - u0))
                    dve.sem_inc(evac_done, 1)

                def hidden_out(u, s):
                    b = s % 2
                    dve.wait_ge(silu_done, u + (1 + m0 - u0))
                    nc.vector.tensor_tensor(GU[:, b, 1, :], GU[:, b, 1, :], SG[:, b, :], ALU.mult).then_inc(h_done, 1)
                    dve.wait_ge(hh_ready, u + (1 + m0 - u0))
                    m = u - u0
                    if isinstance(m, int):
                        d, a, c = HL[:, m, :], GU[:, b, 1, :], HH[:, m, :]
                    else:
                        d, a, c = HL[:, bass.ds(m, 1), :], GU[:, b, 1:2, :], HH[:, bass.ds(m, 1), :]
                    nc.vector.tensor_tensor(d, a, c.bitcast(F32), ALU.subtract).then_inc(hl_ready, 1)

                def step(u, s, n):
                    hidden_in(u, s)
                    split_lo(u + 2, (s + 2) % 4, n)
                    hidden_out(u, s)

                split_lo(u0 + 2, (u0 + 2) % 4, UNIT)
                rstd(2 + 2 * layer, False)
                dve.wait_ge(rs_done, 3 + 2 * layer)
                hidden_in(u0, u0 % 4)
                hidden_out(u0, u0 % 4)
                over_units(dve, u0 + 1, N_GU - 6, lambda u, s: step(u, s, UNIT))
                for u in range(u0 + N_GU - 5, u0 + N_GU):
                    step(u, u % 4, width(u + 2))

            def down(u0):
                layer = 0 if u0 == U_DNA else 1
                g0 = first_group(u0)
                c = VEC["kv_norm"]
                gains = vec[:, c:c + KD] if layer == 0 else gfp[:, :]

                def tile(a, m):
                    if isinstance(m, int):
                        return a[:, m:m + 1] if a is gains else a[:, m:m + 1, :]
                    return a[:, bass.ds(m, 1)] if a is gains else a[:, bass.ds(m, 1), :]

                def half(u, s, n, m):
                    odd = (s - u0) % 2 == 1
                    turn = ((s - u0) % 4) // 2
                    count = m + (8 + 16 * layer + 1)
                    if odd:
                        dve.wait_ge(unit_done, u + 1)
                        src = PROJ[(g0 + turn) % 2][:, 0:T].rearrange("p (a b) -> p a b", a=1)
                        nc.vector.tensor_tensor(tile(X, m), tile(X, m), src, ALU.add).then_inc(x_done, 1)
                        dve.wait_ge(x_done, count)
                        dve.sem_inc(evac_done, 1)
                    if n:
                        split_lo(u + 2, (s + 2) % 4, n)
                    if odd:
                        dve.wait_ge(xh_ready, m + (16 + 16 * layer + 1))
                        nc.vector.scalar_tensor_tensor(tile(XL, m), tile(X, m), tile(gains, m), tile(XH, m).bitcast(F32),
                                                       ALU.mult, ALU.subtract).then_inc(xl_ready, 1)

                with dve.Fori(0, N_DN // 4 - 1) as i:
                    for j in range(4):
                        half(i * 4 + (u0 + j), (u0 + j) % 4, DN_TILES * P, i * 2 + j // 2)
                for j in range(N_DN - 4, N_DN):
                    u = u0 + j
                    half(u, u % 4, width(u + 2) if u + 2 < N_UNITS else 0, j // 2)

            def unit_k(u):
                j = K_UNITS.index(u)
                if j == 0:
                    rstd(3, True)
                scaled(u, KT[:, 2 * j:2 * j + 2, :], 3)

            def unit_q(u):
                j = Q_UNITS.index(u)
                scaled(u, QT[:, 2 * j:2 * j + 2, :], 3, SCALE)

            def unit_v(u):
                j = V_UNITS.index(u)
                values(u, lambda i: V[:, i, j * T:(j + 1) * T], 3)

            def esplit(part):
                c = VEC["b_norm_mix"]
                for k in range(4 * part, 4 * part + 4):
                    dve.wait_ge(eh_ready, 8 + k + 1)
                    lower(HL[:, 8 + k, :], X[:, k, :], vec[:, c + k:c + k + 1], HH[:, 8 + k, :]).then_inc(el_ready, 1)

            def logits(g):
                dve.wait_ge(att_logits, g + 1)
                link(nc.vector.tensor_reduce(MX[:, g % 2, :], LOG[g % 2][:, :].rearrange("p (a b) -> p a b", a=2), AX_X, ALU.max))
                need(dve, att_exp, g - 1)
                nc.vector.tensor_scalar(NM[:, g % 2, :], MX[:, g % 2, :], -1.0, None, ALU.mult).then_inc(att_max, 1)

            def soft(g):
                dve.wait_ge(att_exp, g + 1)
                link(nc.vector.reciprocal(RC[:, g % 2, :], SM[:, g % 2, :]))
                for i in range(2):
                    last = nc.vector.tensor_scalar(PR[:, g % 2, i, :], PR[:, g % 2, i, :], RC[:, g % 2, i:i + 1], None, ALU.mult)
                last.then_inc(att_norm, 1)

            def pv(g):
                if g % 2:
                    t = SBT + (g % 4) // 2
                    base = 0 if g < 4 else 14
                    dve.wait_ge(mh_ready, base + (g % 4) // 2 + 1)
                    lower(HL[:, t, :], OUTP[(g // 2) % 2][:, 0:T], None, HH[:, t, :]).then_inc(ml_ready, 1)
                    dve.wait_ge(ml_ready, base + (g % 4) // 2 + 1)
                    dve.sem_inc(att_out, 1)

            def sbz(h):
                dve.wait_ge(sb_ln, h + 1)
                S = SP[:, h % 2, :]
                need(dve, sb_wt, h - 1)
                link(nc.vector.scalar_tensor_tensor(S, LOG[h % 2][:, 0:3 * P], 0.0, LG[:, h % 2, :], ALU.max, ALU.add))
                nc.vector.tensor_tensor(S[:, 0:2 * P], S[:, 0:2 * P], before[:, :], ALU.mult).then_inc(sb_sp, 1)

            def sbcum(h):
                dve.wait_ge(sb_cum, h + 1)
                nc.vector.tensor_tensor(SP[:, h % 2, :], LOG[h % 2][:, 0:3 * P], notbefore[:, :], ALU.add).then_inc(sb_arg, 1)

            def sbpv(h):
                if h % 2:
                    dve.wait_ge(mh_ready, 8 + h // 2 + 1)
                    lower(HL[:, h // 2, :], OUTP[(h // 2) % 2][:, 0:T], None, HH[:, h // 2, :]).then_inc(ml_ready, 1)
                    dve.wait_ge(ml_ready, 8 + h // 2 + 1)
                    dve.sem_inc(sb_out, 1)

            def consts():
                dve.wait_ge(const_done, 1)
                dve.wait_ge(vecs_in, 16)

            def table_():
                for stage in STAGE:
                    last = nc.vector.memset(stage, NEG)
                link(last)
                dve.wait_ge(buckets_in, 32)
                nc.vector.tensor_copy(RBX, RB.unsqueeze(2).to_broadcast([32, 8, P])).then_inc(table_in, 1)
                dve.wait_ge(table_done, 1)
                for n, bank in enumerate((LOG[0], LOG[1], TRA, OUTP[1])):
                    nc.vector.tensor_copy(STAGE[n][:, :, 0:T], bank[:, :].rearrange("p (a b) -> p a b", a=2)).then_inc(table_out, 1)

            fills = turns()

            def full(b):
                fills[b] += 1
                dve.wait_ge(filled[b], fills[b])

            def skip(*banks):
                for b in banks:
                    fills[b] += 1

            def halves(a):
                return a.rearrange("p (a b) -> p a b", a=2)

            def quarters(a):
                return a.rearrange("p (h i c) -> p h i c", h=2, i=2)

            def h_():
                dve.wait_ge(rs_done, 6)
                dve.wait_ge(xh_ready, 40)
                dve.wait_ge(sq_done, 48)
                for m in range(KD):
                    c = VEC["final_norm"] + m
                    nc.vector.scalar_tensor_tensor(X[:, m, :], X[:, m, :], vec[:, c:c + 1], RS[:, 1, 0, :], ALU.mult,
                                                   ALU.mult).then_inc(h_ready, 1)

            def rw_first():
                split_lo(U_RW + 2, (U_RW + 2) % 4, UNIT)
                split_lo(U_RW + 3, (U_RW + 3) % 4, UNIT)
                rstd(6, True)
                dve.wait_ge(rs_done, 7)
                nc.vector.tensor_tensor(RS[:, 0, :, :], RS[:, 0, :, :], RS[:, 1, :, :], ALU.mult).then_inc(rsp_done, 1)
                nc.vector.tensor_tensor(RSC[:, 0, :], RSC[:, 0, :], RSC[:, 1, :], ALU.mult).then_inc(rsp_done, 1)
                dve.wait_ge(rsp_done, 2)
                nc.vector.memset(C[:, :, 0:1], 0.0)
                take(U_RW, C[:, 0:2, 1:])
                take(U_RW + 1, C[:, 2:4, 1:])

            def take(u, dst, factor=None):
                dve.wait_ge(unit_done, u + 1)
                if factor is None:
                    ins = nc.vector.tensor_tensor(dst, halves(bank_of(u)), RS[:, 0, :, :], ALU.mult)
                else:
                    ins = nc.vector.scalar_tensor_tensor(dst, halves(bank_of(u)), factor, RS[:, 0, :, :], ALU.mult, ALU.mult)
                ins.then_inc(evac_done, 1)

            def unit_rw(u):
                j = 2 * (u - U_RW)
                take(u, C[:, j:j + 2, 1:])
                ahead(u)

            def unit_lr(u):
                dve.wait_ge(unit_done, u + 1)
                nc.vector.tensor_tensor(C[:, 16, 1:], bank_of(u)[:, 0:T], RS[:, 0, 0, :], ALU.mult).then_inc(evac_done, 1)
                ahead(u)

            def shift(part):
                a, b = (4 * part, 4 * part + 4) if part < 4 else (16, 17)
                dve.wait_ge(evac_done, first_group(U_RW + 2 * part + 1 if part < 4 else U_LR) + 1)
                link(nc.vector.tensor_tensor(TMP[:, 0:b - a, :], C[:, a:b, 0:T], C[:, a:b, 1:], ALU.subtract))
                for t in range(a, b):
                    c = VEC["mu_shift_2"] + t
                    last = nc.vector.scalar_tensor_tensor(C[:, t, 1:], TMP[:, t - a, :], vec[:, c:c + 1], C[:, t, 1:],
                                                          ALU.mult, ALU.add)
                last.then_inc(shifted, 1)
                dve.wait_ge(shifted, part + 1)

            def low():
                skip(LOG0, LOG1, OUT0, OUT1)
                dve.wait_ge(taken[LOG0], fills[LOG0])
                dve.wait_ge(taken[LOG1], fills[LOG1])
                dve.wait_ge(masks_in, 16)
                carry = cmask[:, MASKS.index("carry0"):MASKS.index("carry0") + 2, :].rearrange("p a b -> p (a b)")
                for ct in range(4):
                    last = nc.vector.tensor_tensor_scan(CUM[:, ct, :], carry, SW[:, ct, :], 0.0, ALU.mult, ALU.add)
                link(last)
                nc.vector.tensor_tensor(SW[:, :, :], CUM[:, :, :], SW[:, :, :], ALU.subtract).then_inc(cum_done, 1)

            def per_tile(dst, src, name, op=ALU.mult, op1=None, scalar=None):
                for ct in range(4):
                    c = VEC[name] + ct
                    if op1 is None:
                        last = nc.vector.tensor_scalar(dst(ct), src(ct), vec[:, c:c + 1], None, op)
                    else:
                        last = nc.vector.tensor_scalar(dst(ct), src(ct), scalar, vec[:, c:c + 1], op, op1)
                return last

            def kk():
                link(per_tile(lambda ct: KK[:, ct, :], lambda ct: C[:, 4 + ct, 1:], "k_k_2"))
                nc.vector.tensor_tensor(TMP[:, :, :], KK[:, :, :], KK[:, :, :], ALU.mult).then_inc(kk_sq, 1)
                for n, b in enumerate((LOG0, LOG1)):
                    full(b)
                    nc.vector.tensor_scalar(TMP[:, 2 * n:2 * n + 2, :], halves(ps[b][:, :]), 1e-24, None,
                                            ALU.max).then_inc(taken[b], 1)
                dve.wait_ge(taken[LOG0], fills[LOG0])
                dve.wait_ge(taken[LOG1], fills[LOG1])
                nc.vector.reciprocal(TMP[:, :, :], TMP[:, :, :]).then_inc(kk_rv, 1)
                dve.wait_ge(kk_rn, 1)
                link(nc.vector.tensor_tensor(KK[:, :, :], KK[:, :, :], TMP[:, :, :], ALU.mult))
                dve.wait_ge(taken[OUT0], fills[OUT0])
                dve.wait_ge(taken[OUT1], fills[OUT1])
                link(per_tile(lambda ct: TMP[:, ct, :], lambda ct: AI[:, ct, :], "k_a_2", ALU.subtract, ALU.mult, 1.0))
                link(nc.vector.scalar_tensor_tensor(C[:, 4:8, 1:], TMP[:, :, :], 1.0, C[:, 4:8, 1:], ALU.add, ALU.mult))
                link(nc.vector.tensor_tensor(AI[:, :, :], KK[:, :, :], AI[:, :, :], ALU.mult))
                link(nc.vector.tensor_tensor(TMP[:, :, :], C[:, 0:4, 1:], C[:, 4:8, 1:], ALU.mult))
                per_tile(lambda ct: TMP[:, ct, :], lambda ct: TMP[:, ct, :], "r_k_2").then_inc(bon_in, 1)

            def bonus():
                for n, b in enumerate((LOG0, LOG1)):
                    full(b)
                    nc.vector.tensor_tensor(BON[:, 2 * n:2 * n + 2, :], halves(ps[b][:, :]),
                                            C[:, 8 + 2 * n:10 + 2 * n, 1:], ALU.mult).then_inc(taken[b], 1)

            def exps():
                dve.wait_ge(exp_done, 1)
                nc.vector.tensor_tensor(C[:, 0:4, 1:], C[:, 0:4, 1:], TMP[:, :, :], ALU.mult)
                dve.wait_ge(exp_done, 3)
                nc.vector.tensor_tensor(AI[:, :, :], AI[:, :, :], CUM[:, :, :], ALU.mult)
                nc.vector.tensor_tensor(C[:, 4:8, 1:], C[:, 4:8, 1:], CUM[:, :, :], ALU.mult)
                dve.wait_ge(exp_done, 4)
                nc.vector.scalar_tensor_tensor(KK[:, :, :], KK[:, :, :], -1.0, SW[:, :, :], ALU.mult,
                                               ALU.mult).then_inc(hats_done, 1)

            def unit_qa(u):
                j = u - U_QA
                take(u, QA[:, 2 * j:2 * j + 2, :], SCALE)
                ahead(u)

            def unit_ka(u):
                j = u - U_KA
                take(u, KA[:, 2 * j:2 * j + 2, :])
                ahead(u)

            def unit_va(u):
                j = u - U_VA
                values(u, lambda i: VA[:, i, j * T:(j + 1) * T], 6)

            def unit_za(u):
                j = u - U_ZA
                take(u, ZA[:, 2 * j:2 * j + 2, :])
                dve.wait_ge(evac_done, first_group(u) + 1)
                dve.sem_inc(za_in, 1)
                ahead(u)

            def unit_gate(u):
                j = u - U_GATE
                take(u, SGT[:, 2 * j:2 * j + 2, :])
                dve.wait_ge(evac_done, first_group(u) + 1)
                dve.sem_inc(gates_in, 1)
                ahead(u)

            def mlog(h):
                b = (LOG0, LOG1)[h % 2]
                full(b)
                dve.wait_ge(bias_in[h % 2], 32 * (h // 2 + 1))
                if h >= 2:
                    dve.wait_ge(filled[TR], h - 1)
                nc.vector.tensor_tensor(PR[:, h % 2, :, :], halves(ps[b][:, :]), BI[:, h % 2, :, :],
                                        ALU.add).then_inc(taken[b], 1)
                dve.wait_ge(taken[b], fills[b])
                link(nc.vector.tensor_reduce(MX[:, h % 2, :], PR[:, h % 2, :, :], AX_X, ALU.max))
                nc.vector.tensor_scalar(NM[:, h % 2, :], MX[:, h % 2, :], -1.0, None, ALU.mult).then_inc(own_max, 1)

            def msoft(h):
                dve.wait_ge(own_exp, h + 1)
                link(nc.vector.reciprocal(RC[:, h % 2, :], SM[:, h % 2, :]))
                for i in range(2):
                    last = nc.vector.tensor_scalar(PR[:, h % 2, i, :], PR[:, h % 2, i, :], RC[:, h % 2, i:i + 1], None, ALU.mult)
                last.then_inc(own_norm, 1)

            def mturn(h):
                skip(TR)

            def mpv(h):
                b = (OUT0, OUT1)[(h // 2) % 2]
                full(b)
                if h % 2:
                    t = h // 2
                    dve.wait_ge(za_done, t // 2 + 1)
                    nc.vector.tensor_tensor(ZA[:, t, :], ps[b][:, 0:T], ZA[:, t, :], ALU.mult).then_inc(own_y, 1)
                    dve.wait_ge(own_y, t + 1)
                    dve.sem_inc(taken[b], 2)
                    dve.wait_ge(yah_ready, t + 1)
                    lower(YAL[:, t, :], ZA[:, t, :], None, YAH[:, t, :]).then_inc(yal_ready, 1)

            def tok(ct):
                skip(TR, OUT0)
                if ct == 0:
                    nc.vector.memset(TTB[:, :, :], 0.0)

            def grams(ct):
                need(dve, y_out, ct)
                for hh in range(2):
                    b = (LOG0, LOG1)[hh]
                    full(b)
                    nc.vector.tensor_tensor(AM[:, hh, :, :], halves(ps[b][:, 0:T]), mask("strict_lower", 2), ALU.mult)
                    nc.vector.tensor_tensor(NN[:, hh, :, :], halves(ps[b][:, T:]), mask("pair_upper", 2),
                                            ALU.mult).then_inc(taken[b], 1)
                    b = (OUT0, OUT1)[hh]
                    full(b)
                    nc.vector.tensor_tensor(LK[:, hh, :, :], halves(ps[b][:, 0:T]), mask("strict_upper", 2), ALU.mult)
                    nc.vector.tensor_tensor(MB[:, hh, :, :], halves(ps[b][:, T:]), mask("upper", 2),
                                            ALU.mult).then_inc(taken[b], 1)
                    b = (TR, ST)[hh]
                    full(b)
                    nc.vector.tensor_tensor(MC[:, hh, :, :], halves(ps[b][:, 0:T]), mask("upper", 2),
                                            ALU.mult).then_inc(taken[b], 1)
                for b in (LOG0, LOG1):
                    dve.wait_ge(taken[b], fills[b])
                for hh in range(2):
                    last = nc.vector.tensor_tensor(MM[:, hh, :, :], AM[:, hh, :, :], mask("pair_lower", 2), ALU.mult)
                link(last)
                eye = ident[:, :].unsqueeze(1).to_broadcast([P, 2, P])
                for hh in range(2):
                    nc.vector.tensor_tensor(NN[:, hh, :, :], NN[:, hh, :, :], eye, ALU.add)
                    nc.vector.tensor_tensor(MM[:, hh, :, :], MM[:, hh, :, :], eye, ALU.add).then_inc(inverse_done, 1)

            def lv(ct):
                skip(ST)

            def level(ct, lvl):
                join = mask(f"join{2 << lvl}", 2)
                for hh, b in ((0, LOG0), (1, LOG1)):
                    full(b)
                    nc.vector.tensor_tensor(YM[:, hh, :, :], halves(ps[b][:, 0:T]), join, ALU.mult).then_inc(taken[b], 1)
                for hh, b in ((0, OUT0), (1, OUT1)):
                    dve.wait_ge(taken[b], fills[b])
                    if lvl == 0:
                        dve.wait_ge(inverse_done, 2 * ct + hh + 1)
                    full(b)
                    last = nc.vector.tensor_tensor(NN[:, hh, :, :], NN[:, hh, :, :], halves(ps[b][:, 0:T]), ALU.add)
                    if lvl < 4:
                        last = nc.vector.tensor_tensor(MM[:, hh, :, :], MM[:, hh, :, :], halves(ps[b][:, T:]), ALU.add)
                    last.then_inc(taken[b], 1)

            def apply(ct):
                skip(LOG0, TR)

            def chunks(ct):
                skip(LOG1, OUT0)

            def scan(ct, c):
                if c == 1:
                    dve.wait_ge(taken[LOG1], fills[LOG1])
                    dve.wait_ge(taken[OUT0], fills[OUT0])
                    src = GT[:, 0, 1, :]
                    dve.sem_inc(state_done, 1)
                else:
                    full(LOG0)
                    for hh in range(2):
                        o = slice(hh * HALF, (hh + 1) * HALF)
                        last = nc.vector.tensor_tensor(TTS[o, :], ps[LOG0][o, 0:HALF], TTB[o, c - 1, o], ALU.add)
                    last.then_inc(taken[LOG0], 1)
                    dve.wait_ge(taken[LOG0], fills[LOG0])
                    link(nc.vector.tensor_tensor(TTS[:, :], TTS[:, :], GT[:, c - 1, 1, :], ALU.add))
                    src = TTS[:, :]
                for hh in range(2):
                    o = slice(hh * HALF, (hh + 1) * HALF)
                    last = nc.vector.tensor_scalar(TTB[o, c, o], src[o, :], ED[o, ct, c - 1:c], None, ALU.mult)
                last.then_inc(state_done, 1)
                dve.wait_ge(state_done, 4 * ct + c + 1)

            def sa(ct):
                for hh, b in ((0, OUT1), (1, ST)):
                    full(b)
                    nc.vector.tensor_tensor(SAO[:, hh, :, :], halves(ps[b][:, 0:P]), AM[:, hh, :, HALF:P],
                                            ALU.add).then_inc(taken[b], 1)

            def yt(ct):
                skip(LOG1)

            def gn(ct):
                y = KK[:, ct, :]
                full(TR)
                nc.vector.scalar_tensor_tensor(y, ps[TR][:, 0:T], -1.0 / HALF, y, ALU.mult, ALU.add).then_inc(taken[TR], 1)
                dve.wait_ge(taken[TR], fills[TR])
                nc.vector.tensor_tensor(YQ[:, :], y, y, ALU.mult).then_inc(gn_sq, 1)

            def gn2(ct):
                full(TR)
                nc.vector.tensor_scalar(YQ[:, :], ps[TR][:, 0:T], 1.0 / HALF, GN_EPS, ALU.mult, ALU.add).then_inc(taken[TR], 1)
                dve.wait_ge(taken[TR], fills[TR])
                nc.vector.reciprocal(YQ[:, :], YQ[:, :]).then_inc(gn_rv, 1)

            def gn3(ct):
                y = KK[:, ct, :]
                dve.wait_ge(gn_rs, ct + 1)
                link(nc.vector.tensor_tensor(y, y, YQ[:, :], ALU.mult))
                w, b = VEC["ln_x_w_2"] + ct, VEC["ln_x_b_2"] + ct
                link(nc.vector.tensor_scalar(y, y, vec[:, w:w + 1], vec[:, b:b + 1], ALU.mult, ALU.add))
                link(nc.vector.tensor_tensor(y, y, BON[:, ct, :], ALU.add))
                dve.wait_ge(z_done, 1)
                nc.vector.tensor_tensor(y, y, C[:, 12 + ct, 1:], ALU.mult).then_inc(yb_done, 1)
                dve.wait_ge(ybh_ready, ct + 1)
                lower(YBL[:, ct, :], y, None, YBH[:, ct, :]).then_inc(ybl_ready, 1)

            def unit_pab(u):
                j = u - U_PAB
                g = first_group(u)
                dve.wait_ge(unit_done, u + 1)
                dve.wait_ge(gates_done, 8)
                a, b = SGT[:, 2 * j:2 * j + 2, :], SGT[:, 8 + 2 * j:10 + 2 * j, :]
                nc.vector.tensor_tensor(a, halves(PROJ[g % 2][:, :]), a, ALU.mult).then_inc(evac_done, 1)
                nc.vector.tensor_tensor(b, halves(PROJ[(g + 1) % 2][:, :]), b, ALU.mult).then_inc(evac_done, 1)
                dve.wait_ge(evac_done, g + 2)
                nc.vector.tensor_tensor(a, a, b, ALU.add).then_inc(merged, 1)
                ahead(u)
                dve.wait_ge(merged, j + 1)
                for m in (2 * j, 2 * j + 1):
                    dve.wait_ge(xh_ready, 40 + m + 1)
                    lower(XL[:, m, :], SGT[:, m, :], None, XH[:, m, :]).then_inc(xl_ready, 1)

            def unit_out2(u):
                j = u - U_OUT2
                dve.wait_ge(unit_done, u + 1)
                nc.vector.tensor_copy(SGT[:, 8 + 2 * j:10 + 2 * j, :], halves(bank_of(u))).then_inc(evac_done, 1)
                ahead(u)

            def p_in_():
                for k in range(2):
                    dve.wait_ge(ph_ready, k + 1)
                    lower(PL[:, k, :], PIN[:, k, :], None, PH[:, k, :]).then_inc(pl_ready, 1)

            def unit_eup(u):
                g = first_group(u)
                for j in range(4):
                    if j < 3:
                        dve.wait_ge(e_part, j + 1)
                    else:
                        dve.wait_ge(unit_done, u + 1)
                    nc.vector.tensor_copy(SGT[:, 2 * j:2 * j + 2, :], halves(PROJ[(g + j) % 2][:, :])).then_inc(evac_done, 1)
                ahead(u)

            def post():
                dve.wait_ge(rs_done, 8)
                for m in range(KD):
                    c = VEC["g_post_2"] + m
                    nc.vector.scalar_tensor_tensor(SGT[:, 8 + m, :], SGT[:, 8 + m, :], vec[:, c:c + 1], RS[:, 1, 0, :],
                                                   ALU.mult, ALU.mult).then_inc(y_done, 1)
                for m in range(KD):
                    dve.wait_ge(y_done, 8)
                    nc.vector.tensor_tensor(X[:, m, :], X[:, m, :], SGT[:, 8 + m, :], ALU.add).then_inc(y_done, 1)
                for m in range(KD):
                    dve.wait_ge(xh_ready, 48 + m + 1)
                    lower(XL[:, m, :], X[:, m, :], None, XH[:, m, :]).then_inc(xl_ready, 1)

            def unit_egate(u):
                j = u - U_EGATE
                s = SIG[:, j % 2, :, :]
                dve.wait_ge(sig_done, j + 1)
                dve.sem_inc(evac_done, 1)
                link(nc.vector.tensor_tensor(s, s, SGT[:, 2 * j:2 * j + 2, :], ALU.mult))
                x = X[:, 2 * j:2 * j + 2, :]
                nc.vector.tensor_tensor(x, x, s, ALU.add).then_inc(out_ready, 1)
                ahead(u)

            run({
                "h": h_, "rw_first": rw_first, "unit_rw": unit_rw, "unit_lr": unit_lr, "shift": shift, "low": low, "kk": kk,
                "bonus": bonus, "exps": exps, "unit_qa": unit_qa, "unit_ka": unit_ka, "unit_va": unit_va,
                "unit_za": unit_za, "unit_gate": unit_gate, "mlog": mlog, "msoft": msoft, "mturn": mturn, "mpv": mpv,
                "tok": tok, "grams": grams, "lv": lv, "level": level, "apply": apply, "chunks": chunks, "scan": scan,
                "sa": sa, "yt": yt, "gn": gn, "gn2": gn2, "gn3": gn3, "unit_pab": unit_pab, "unit_out2": unit_out2, "p_in": p_in_,
                "unit_eup": unit_eup, "post": post, "unit_egate": unit_egate,
                "consts": consts, "table": table_, "pads": pads, "split": lambda u: split_lo(u, u % 4, UNIT),
                "mem_in": mem_in_, "x_in": x_in_, "unit_mk": unit_mk, "unit_mv": unit_mv,
                "stats": lambda n, c: rstd(n, c) if n in (1, 5, 7) else None,
                "unit_qm": unit_qm, "unit_pool": unit_pool, "pool": pool, "grouped": grouped,
                "unit_out": unit_out, "xsplit": lambda layer: xlower(layer, 6), "gu": gu, "down": down,
                "unit_k": unit_k, "unit_q": unit_q, "unit_v": unit_v, "esplit": esplit,
                "logits": logits, "soft": soft, "pv": pv, "sbz": sbz, "sbcum": sbcum, "sbpv": sbpv,
            })

        @block.gpsimd
        def _(pool):
            chain = [0]

            def link(ins):
                chain[0] += 1
                ins.then_inc(pool_chain, 1)
                pool.wait_ge(pool_chain, chain[0])

            def consts():
                nc.gpsimd.memset(ones[:, :], 1.0)
                nc.gpsimd.memset(nones[:, :], -1.0)
                nc.gpsimd.memset(before[:, :], 1.0)
                link(nc.gpsimd.memset(notbefore[:, :], 0.0))
                nc.gpsimd.affine_select(ident[:, :], ones[:, :], [[-1, P]], ALU.is_equal, 0.0, base=0, channel_multiplier=1)
                nc.gpsimd.affine_select(ntri[:, :], nones[:, :], [[-1, P]], ALU.is_ge, 0.0, base=0, channel_multiplier=1)
                nc.gpsimd.affine_select(before[:, :], before[:, :], [[0, 2], [1, P]], ALU.is_gt, 0.0, base=0,
                                        channel_multiplier=-1)
                nb = notbefore[:, 0:2 * P]
                link(nc.gpsimd.affine_select(nb, nb, [[0, 2], [1, P]], ALU.is_gt, NEG, base=0, channel_multiplier=-1))
                pool.sem_inc(const_done, 1)

                pool.dma_start(RB[:, :], io["rel_bias"]).then_inc(buckets_in, 16)
                pool.dma_start(OH[:, :], io["buckets"]).then_inc(buckets_in, 16)

            def table_():
                for n in range(4):
                    pool.wait_ge(table_out, n + 1)
                    pool.dma_start(table[2 * n:2 * n + 2, :, :].rearrange("h p n -> p h n"), STAGE[n]).then_inc(table_stored, 16)
                pool.wait_ge(table_stored, 64)
                nc.gpsimd.iota(INV[:, :, :], [[0, 4], [1, T]], base=1, channel_multiplier=0,
                               allow_small_or_imprecise_dtypes=True).then_inc(const_done, 1)

            def squares(n, m, src):
                h = m % 2
                if m == 0:
                    need(pool, stat_done, n)
                if m < 2:
                    nc.gpsimd.tensor_tensor(ACC[:, h, :], src, src, ALU.mult).then_inc(sq_done, 1)
                else:
                    link(nc.gpsimd.tensor_tensor(SQT[:, h, :], src, src, ALU.mult))
                    pool.wait_ge(sq_done, 8 * n + m)
                    nc.gpsimd.tensor_tensor(ACC[:, h, :], ACC[:, h, :], SQT[:, h, :], ALU.add).then_inc(sq_done, 1)

            def mem_in_():
                pool.wait_ge(mem_in, 16)
                for m in range(KD):
                    squares(0, m, MEM[:, m, :])

            def x_in_():
                pool.wait_ge(x_in, 16)
                for m in range(KD):
                    squares(1, m, X[:, m, :])

            def residual(n, base):
                def tiles(*_):
                    for m in range(KD):
                        pool.wait_ge(x_done, base + m + 1)
                        squares(n, m, X[:, m, :])
                return tiles

            def h_():
                for m in range(KD):
                    pool.wait_ge(h_ready, m + 1)
                    squares(6, m, X[:, m, :])
                pool.wait_ge(unit_done, U_RW)
                pool.dma_start(cmask[:, :, :], io["masks"]).then_inc(masks_in, 16)
                pool.dma_start(low_up[:, :], io["low_up"]).then_inc(low_in, 16)

            def bias(h):
                if h >= 2:
                    pool.wait_ge(own_max, h - 1)
                for i in range(2):
                    src = bass.AP(table.tensor, h * P * 2 * T + T - 1 - i * P, [[2 * T - 1, P], [1, T]])
                    dst = BI[:, h % 2, i, :]
                    if i == 0:
                        pool.dma_start(dst, src).then_inc(bias_half[h % 2], 16)
                    else:
                        pool.dma_start(dst, src).then_inc(bias_in[h % 2], 16)

            def out2(u):
                if u == U_OUT2 + 3:
                    for m in range(KD):
                        pool.wait_ge(evac_done, first_group(U_OUT2 + m // 2) + 1)
                        squares(7, m, SGT[:, 8 + m, :])
                elif u == U_OUT2:
                    pool.wait_ge(ybh_ready, 4)
                    pool.wait_ge(ybl_ready, 4)
                    pool.dma_start(PIN[:, :, :], io["p"]).then_inc(p_in, 16)

            run({
                "h": h_, "mlog": bias, "unit_out2": out2,
                "consts": consts, "table": table_, "mem_in": mem_in_, "x_in": x_in_,
                "xsplit": lambda layer: residual(2 + 2 * layer, 16 * layer)(),
                "down": lambda u0: residual(3 if u0 == U_DNA else 5, 8 if u0 == U_DNA else 24)(),
            })


def tiles(w):
    k, m = w.shape
    return w.reshape(k // P, P, m // P, P).transpose(0, 2, 1, 3)


def channel_units(w):
    t = tiles(w).transpose(1, 0, 2, 3)
    return t.reshape(-1, 16, P, P).transpose(0, 2, 1, 3).reshape(-1, P, UNIT)


def token_units(w):
    t = tiles(w)
    k, m = t.shape[:2]
    return t.reshape(k, m // 2, 2, P, P).transpose(1, 3, 0, 2, 4).reshape(-1, P, UNIT)


def ffn_units(w):
    t = tiles(w).transpose(1, 0, 2, 3)
    return np.stack([t[:KF], t[KF:]], 1).reshape(KF, 16, P, P).transpose(0, 2, 1, 3).reshape(-1, P, UNIT)


def down_units(w):
    t = tiles(w).transpose(1, 0, 2, 3)
    return t.reshape(N_DN, DN_TILES, P, P).transpose(0, 2, 1, 3).reshape(-1, P, DN_TILES * P)


def columns(v):
    return v.reshape(-1, P).T


def on_channels(x):
    return np.ascontiguousarray(x.reshape(T, -1, P).transpose(2, 1, 0))


def layout(i):
    h = 4 * HALF
    akv, bkv, kv, q, win, w2 = (i["a_w_mem_kv"][0], i["b_w_mem_kv"][0], i["w_kv"], i["b_w_q"][0], i["a_w_in"][0],
                                i["w_in_2"][0])
    sbw = NSB * HALF
    c = np.cumsum([0, 512, 512, 512, 512, 2048, 128, 1024, 1024])
    qa, ka, va, za, rw, lr, ga, gb = (w2[:, c[j]:c[j + 1]] for j in range(8))
    low = tiles(lr).transpose(1, 0, 2, 3).reshape(8, P, P).transpose(1, 0, 2).reshape(1, P, KD * P)
    pab = np.concatenate([i["p_a_2"][0], i["p_b_2"][0]], 0)
    up = tiles(i["w_ple_up_2"][0]).transpose(1, 0, 2, 3).reshape(1, 16, P, P).transpose(0, 2, 1, 3).reshape(1, P, UNIT)
    sb_units = {"k": channel_units(kv[:, :sbw]), "q": channel_units(q[:, :sbw]), "m": channel_units(q[:, sbw:]),
                "v": token_units(kv[:, sbw:])}
    wide = [channel_units(akv[:, :h]), token_units(akv[:, h:]),
            channel_units(win[:, sbw:]), channel_units(win[:, :sbw]),
            channel_units(bkv[:, :h]), token_units(bkv[:, h:]), channel_units(i["a_w_out"][0]),
            ffn_units(i["a_w_gu"][0]), *[sb_units[kind][SB_ORDER[:n].count(kind)][None] for n, kind in enumerate(SB_ORDER)],
            channel_units(i["b_w_out"][0]), ffn_units(i["b_w_gu"][0]),
            channel_units(rw), np.concatenate([low, np.zeros((1, P, KD * P), low.dtype)], 2), channel_units(qa),
            channel_units(ka), token_units(va), channel_units(za), channel_units(ga), channel_units(gb),
            channel_units(pab), channel_units(i["w_out_2"][0]), up, channel_units(i["w_ple_gate_2"][0])]
    group = np.zeros((8, P, 192), np.float32)
    for g in range(4):
        group[2 * g:2 * g + 2].reshape(2 * P, 192)[HALF * (g % 2):][:192] = i["a_w_group"][0, g]
    down = [down_units(i["a_w_down"][0]), down_units(i["b_w_down"][0])]
    return {
        "wide": np.ascontiguousarray(np.concatenate(wide, 0)),
        "down": np.ascontiguousarray(np.concatenate(down, 0)),
        "vec": np.ascontiguousarray(np.concatenate([columns(i[n].reshape(-1)) for n in VEC], 1)),
        "x": on_channels(i["x"][0]), "mem": on_channels(i["mem"][0]), "p": on_channels(i["p_2"][0, 0]),
        "group": np.ascontiguousarray(group.transpose(1, 0, 2)),
        "low_up": np.ascontiguousarray(np.concatenate([i["w_up_2"][0], i["a_up_2"][0]], 0)),
        "masks": masks(), "buckets": buckets(),
        "rel_bias": np.ascontiguousarray(i["rel_bias_2"]),
    }


def kernel(**inputs):
    import concourse.bacc as bacc
    from concourse.bass_utils import run_bass_kernel_spmd

    nc = bacc.Bacc("TRN2", target_bir_lowering=False, num_devices=1)
    arrays, io = {}, {}
    for name, a in layout({k: np.asarray(v) for k, v in inputs.items()}).items():
        arrays[f"in_{name}"] = a
        io[name] = nc.dram_tensor(f"in_{name}", a.shape, mybir.dt.from_np(a.dtype), kind="ExternalInput").ap()
    out = nc.dram_tensor("out", (P, KD, T), F32, kind="ExternalOutput").ap()
    program(nc, io, out)
    got = run_bass_kernel_spmd(nc, [arrays], core_ids=[0]).results[0]["out"]
    return np.ascontiguousarray(np.asarray(got).transpose(2, 1, 0).reshape(1, T, D))
```
